# Optimizing a Trainium2 kernel written in Bass

```python
import jax, jax.numpy as jnp
from jax import lax
import numpy as np

D_MODEL = 2048
BATCH = 1
SEQ = 512
DEPTH = 1

GDN_HEADS = 8
GDN_HEAD_DIM = 128
GDN_WIDTH = GDN_HEADS * GDN_HEAD_DIM
GDN_CHUNK = 64
CONV_WIDTH = 4
LRU_WIDTH = 1024
LRU_BLOCKS = 8
LRU_BLOCK_DIM = LRU_WIDTH // LRU_BLOCKS
LRU_C = 8.0
D_FF = 4 * D_MODEL
N_BRANCHES = 2
RMS_EPS = 1e-6
L2_EPS = 1e-6

SPLIT_SIZES = (3 * GDN_WIDTH, GDN_WIDTH, GDN_HEADS, GDN_HEADS, LRU_WIDTH, LRU_WIDTH, D_MODEL, D_MODEL)
IN_COLS = 3 * GDN_WIDTH + GDN_WIDTH + 2 * GDN_HEADS + 2 * LRU_WIDTH + N_BRANCHES * D_MODEL

kernel_name = 'hybrid_gdn_rglru_gated_merge'

def rms_norm(x, gain):
    xf = x.astype(jnp.float32)
    y = xf * lax.rsqrt(jnp.mean(xf * xf, axis=-1, keepdims=True) + RMS_EPS)
    return (y * gain.astype(jnp.float32)).astype(x.dtype)

def l2_normalize(x):
    return x * lax.rsqrt(jnp.sum(x * x, axis=-1, keepdims=True) + L2_EPS)

def causal_depthwise_conv(x, w):
    width = w.shape[0]
    seq = x.shape[1]
    xp = jnp.pad(x, ((0, 0), (width - 1, 0), (0, 0)))
    y = xp[:, 0:seq, :] * w[0]
    for j in range(1, width):
        y = y + xp[:, j:j + seq, :] * w[j]
    return y

def gated_delta_rule_chunked(q, k, v, g, beta):
    bsz, heads, seq, dk = q.shape
    dv = v.shape[-1]
    c = GDN_CHUNK
    n = seq // c
    q = q * (dk ** -0.5)

    def chunks(t):
        return t.reshape((bsz, heads, n, c) + t.shape[3:])

    q, k, v, g, beta = chunks(q), chunks(k), chunks(v), chunks(g), chunks(beta)
    g = jnp.cumsum(g, axis=-1)
    k_beta = k * beta[..., None]
    v_beta = v * beta[..., None]
    causal = jnp.tril(jnp.ones((c, c), dtype=bool))
    strict = jnp.tril(jnp.ones((c, c), dtype=bool), -1)
    diff = g[..., :, None] - g[..., None, :]
    decay = jnp.where(causal, jnp.exp(jnp.where(causal, diff, 0.0)), 0.0)
    lower = jnp.where(strict, jnp.einsum('bhnid,bhnjd->bhnij', k_beta, k) * decay, 0.0)
    eye = jnp.eye(c, dtype=q.dtype)
    t_inv = lax.linalg.triangular_solve(eye + lower, jnp.broadcast_to(eye, lower.shape),
                                        left_side=True, lower=True, unit_diagonal=True)
    u = jnp.einsum('bhnij,bhnjv->bhniv', t_inv, v_beta)
    w = jnp.einsum('bhnij,bhnjk->bhnik', t_inv, k_beta * jnp.exp(g)[..., None])
    qk = jnp.where(causal, jnp.einsum('bhnid,bhnjd->bhnij', q, k) * decay, 0.0)
    q_dec = q * jnp.exp(g)[..., None]
    g_last = g[..., -1]
    k_dec = k * jnp.exp(g_last[..., None] - g)[..., None]

    xs = (jnp.moveaxis(u, 2, 0), jnp.moveaxis(w, 2, 0), jnp.moveaxis(qk, 2, 0),
          jnp.moveaxis(q_dec, 2, 0), jnp.moveaxis(k_dec, 2, 0), jnp.moveaxis(g_last, 2, 0))

    def step(state, inp):
        u_n, w_n, qk_n, qd_n, kd_n, gl_n = inp
        v_new = u_n - jnp.einsum('bhck,bhkv->bhcv', w_n, state)
        out = (jnp.einsum('bhck,bhkv->bhcv', qd_n, state)
               + jnp.einsum('bhij,bhjv->bhiv', qk_n, v_new))
        state = state * jnp.exp(gl_n)[..., None, None] + jnp.einsum('bhck,bhcv->bhkv', kd_n, v_new)
        return state, out

    state0 = jnp.zeros((bsz, heads, dk, dv), dtype=q.dtype)
    _, out = lax.scan(step, state0, xs)
    return jnp.moveaxis(out, 0, 2).reshape(bsz, heads, seq, dv)

def gated_deltanet_branch(qkv, z, a, b, conv_w, a_log, dt_bias, norm_gain):
    bsz, seq, _ = qkv.shape
    f32 = jnp.float32
    qkv = jax.nn.silu(causal_depthwise_conv(qkv, conv_w))
    q, k, v = jnp.split(qkv, 3, axis=-1)

    def to_heads(t):
        return t.reshape(bsz, seq, GDN_HEADS, GDN_HEAD_DIM).transpose(0, 2, 1, 3).astype(f32)

    q = l2_normalize(to_heads(q))
    k = l2_normalize(to_heads(k))
    v = to_heads(v)
    g = -jnp.exp(a_log.astype(f32)) * jax.nn.softplus(a.astype(f32) + dt_bias.astype(f32))
    beta = jax.nn.sigmoid(b.astype(f32))
    o = gated_delta_rule_chunked(q, k, v, g.transpose(0, 2, 1), beta.transpose(0, 2, 1))
    o = rms_norm(o.transpose(0, 2, 1, 3), norm_gain)
    o = o.astype(z.dtype) * jax.nn.silu(z).reshape(bsz, seq, GDN_HEADS, GDN_HEAD_DIM)
    return o.reshape(bsz, seq, GDN_WIDTH)

def rglru_branch(xb, yb, conv_w, conv_b, w_gate_a, b_gate_a, w_gate_x, b_gate_x, lam):
    bsz, seq, _ = xb.shape
    f32 = jnp.float32
    xc = causal_depthwise_conv(xb, conv_w) + conv_b
    xh = xc.reshape(bsz, seq, LRU_BLOCKS, LRU_BLOCK_DIM)
    r = jax.nn.sigmoid(jnp.einsum('bsni,nij->bsnj', xh, w_gate_a).reshape(bsz, seq, LRU_WIDTH) + b_gate_a)
    i = jax.nn.sigmoid(jnp.einsum('bsni,nij->bsnj', xh, w_gate_x).reshape(bsz, seq, LRU_WIDTH) + b_gate_x)
    log_a = -LRU_C * r.astype(f32) * jax.nn.softplus(-lam.astype(f32))
    a = jnp.exp(log_a)
    bterm = jnp.sqrt(-jnp.expm1(2.0 * log_a)) * (i * xc).astype(f32)

    def combine(left, right):
        a_l, b_l = left
        a_r, b_r = right
        return a_l * a_r, a_r * b_l + b_r

    _, h = lax.associative_scan(combine, (a, bterm), axis=1)
    return h.astype(xb.dtype) * jax.nn.gelu(yb)

def hybrid_layer(x, attn_norm, w_in, gdn_conv_w, gdn_a_log, gdn_dt_bias, gdn_norm,
                 lru_conv_w, lru_conv_b, lru_w_a, lru_b_a, lru_w_x, lru_b_x, lru_lambda,
                 w_branch_gdn, w_branch_lru, w_out, mlp_norm, w_up, w_down):
    h = rms_norm(x, attn_norm)
    proj = h @ w_in
    offsets = []
    acc = 0
    for s in SPLIT_SIZES[:-1]:
        acc += s
        offsets.append(acc)
    qkv, z, a, b, xb, yb, gate_gdn, gate_lru = jnp.split(proj, offsets, axis=-1)
    o_gdn = gated_deltanet_branch(qkv, z, a, b, gdn_conv_w, gdn_a_log, gdn_dt_bias, gdn_norm)
    o_lru = rglru_branch(xb, yb, lru_conv_w, lru_conv_b, lru_w_a, lru_b_a, lru_w_x, lru_b_x, lru_lambda)
    merged = (jax.nn.sigmoid(gate_gdn) * (o_gdn @ w_branch_gdn)
              + jax.nn.sigmoid(gate_lru) * (o_lru @ w_branch_lru))
    x = x + merged @ w_out
    h = rms_norm(x, mlp_norm)
    x = x + jnp.square(jax.nn.relu(h @ w_up)) @ w_down
    return x

def setup_inputs(seed: int = 0) -> dict:
    key = jax.random.key(seed)
    ks = jax.random.split(key, 24)
    f32 = jnp.float32
    d, l = D_MODEL, DEPTH

    def normal(k, shape, scale):
        return jax.random.normal(k, shape, f32) * scale

    def gain(k, shape):
        return 1.0 + 0.02 * jax.random.normal(k, shape, f32)

    x = normal(ks[0], (BATCH, SEQ, d), 1.0)
    attn_norm = gain(ks[1], (l, d))
    w_in = normal(ks[2], (l, d, IN_COLS), d ** -0.5)
    gdn_conv_w = normal(ks[3], (l, CONV_WIDTH, 3 * GDN_WIDTH), CONV_WIDTH ** -0.5)
    gdn_a_log = jnp.log(jax.random.uniform(ks[4], (l, GDN_HEADS), f32, 1.0, 16.0))
    dt = jnp.exp(jax.random.uniform(ks[5], (l, GDN_HEADS), f32, np.log(1e-3), np.log(1e-1)))
    gdn_dt_bias = dt + jnp.log(-jnp.expm1(-dt))
    gdn_norm = gain(ks[6], (l, GDN_HEAD_DIM))
    lru_conv_w = normal(ks[7], (l, CONV_WIDTH, LRU_WIDTH), CONV_WIDTH ** -0.5)
    lru_conv_b = normal(ks[8], (l, LRU_WIDTH), 0.01)
    lru_w_a = normal(ks[9], (l, LRU_BLOCKS, LRU_BLOCK_DIM, LRU_BLOCK_DIM), LRU_BLOCK_DIM ** -0.5)
    lru_b_a = normal(ks[10], (l, LRU_WIDTH), 0.01)
    lru_w_x = normal(ks[11], (l, LRU_BLOCKS, LRU_BLOCK_DIM, LRU_BLOCK_DIM), LRU_BLOCK_DIM ** -0.5)
    lru_b_x = normal(ks[12], (l, LRU_WIDTH), 0.01)
    a0 = jax.random.uniform(ks[13], (l, LRU_WIDTH), f32, 0.9, 0.999)
    s0 = a0 ** (1.0 / LRU_C)
    lru_lambda = jnp.log(s0) - jnp.log1p(-s0)
    w_branch_gdn = normal(ks[14], (l, GDN_WIDTH, d), GDN_WIDTH ** -0.5)
    w_branch_lru = normal(ks[15], (l, LRU_WIDTH, d), LRU_WIDTH ** -0.5)
    w_out = normal(ks[16], (l, d, d), d ** -0.5)
    mlp_norm = gain(ks[17], (l, d))
    w_up = normal(ks[18], (l, d, D_FF), d ** -0.5)
    w_down = normal(ks[19], (l, D_FF, d), D_FF ** -0.5)
    final_norm = gain(ks[20], (d,))
    return {'x': x, 'attn_norm': attn_norm, 'w_in': w_in, 'gdn_conv_w': gdn_conv_w,
            'gdn_a_log': gdn_a_log, 'gdn_dt_bias': gdn_dt_bias, 'gdn_norm': gdn_norm,
            'lru_conv_w': lru_conv_w, 'lru_conv_b': lru_conv_b, 'lru_w_a': lru_w_a, 'lru_b_a': lru_b_a,
            'lru_w_x': lru_w_x, 'lru_b_x': lru_b_x, 'lru_lambda': lru_lambda,
            'w_branch_gdn': w_branch_gdn, 'w_branch_lru': w_branch_lru, 'w_out': w_out,
            'mlp_norm': mlp_norm, 'w_up': w_up, 'w_down': w_down, 'final_norm': final_norm}

def reference(x, attn_norm, w_in, gdn_conv_w, gdn_a_log, gdn_dt_bias, gdn_norm,
              lru_conv_w, lru_conv_b, lru_w_a, lru_b_a, lru_w_x, lru_b_x, lru_lambda,
              w_branch_gdn, w_branch_lru, w_out, mlp_norm, w_up, w_down, final_norm):
    for layer in range(DEPTH):
        x = hybrid_layer(x, attn_norm[layer], w_in[layer], gdn_conv_w[layer], gdn_a_log[layer],
                         gdn_dt_bias[layer], gdn_norm[layer], lru_conv_w[layer], lru_conv_b[layer],
                         lru_w_a[layer], lru_b_a[layer], lru_w_x[layer], lru_b_x[layer], lru_lambda[layer],
                         w_branch_gdn[layer], w_branch_lru[layer], w_out[layer], mlp_norm[layer],
                         w_up[layer], w_down[layer])
    return rms_norm(x, final_norm)


_drawn_inputs = setup_inputs


def setup_inputs(seed=0):
    import zlib

    import numpy as np

    out = dict(_drawn_inputs(seed))
    spreads = {}
    factors = {'attn_norm': 4.299,
     'gdn_norm': 22.373,
     'lru_conv_b': 11.395,
     'lru_b_a': 200.0,
     'lru_b_x': 200.0,
     'mlp_norm': 12.624,
     'final_norm': 23.759}
    for name, (base, spread) in spreads.items():
        noise = np.random.default_rng([zlib.crc32(name.encode()), seed]).standard_normal(out[name].shape)
        drawn = base * np.exp(spread * noise) if base else spread * noise
        out[name] = __import__('jax').numpy.asarray(drawn.astype(out[name].dtype))
    for name, factor in factors.items():
        out[name] = (out[name] * factor).astype(out[name].dtype)
    return out
```

```python
from contextlib import ExitStack, contextmanager

import concourse.bass as bass
from concourse import mybir

F32 = mybir.dt.float32
F32R = mybir.dt.float32r
ALU = mybir.AluOpType
ACT = mybir.ActivationFunctionType
ds = bass.ds

P = 128
T = 512
TT = T // P
D = 2048
KT = D // P
HEADS = 8
BW = HEADS * P
GH = 4
GROUPS = HEADS // GH
CONV = 4
FF_PARTS = 4
LEVELS = [1 << n for n in range(7)]
RMS_EPS = 1e-6
L2_EPS = 1e-6
GELU_CUBIC = 0.044715
GELU_SCALE = 0.7978845608028654
QK = P ** -0.5

COL_Q, COL_K, COL_V, COL_Z = 0, BW, 2 * BW, 3 * BW
COL_AB = 4 * BW
COL_XB = COL_AB + 2 * HEADS
COL_YB = COL_XB + BW
COL_GATE = COL_YB + BW

R_ATTN, R_MLP, R_FIN = 0, KT, 2 * KT
R_LCW = 3 * KT
R_LCB = R_LCW + CONV * HEADS
R_BA, R_BX, R_LAM = R_LCB + 8, R_LCB + 16, R_LCB + 24
R_GN = R_LCB + 32
ROWS_A = R_GN + 1
ROWS_B = CONV * 3 * HEADS

RAW, SPLIT = 4, 2
KC = 8
PIECE = KC * P

N_AB, N_QKV, N_UNIT = 0, 2, 2 + 48
N_Z = N_UNIT + 96
N_MERGE = N_Z + 16
N_OUT = N_MERGE + 32
N_MLP = N_OUT + 32
N_PART = 64
UNIT_LINKS = 18
M_AB, M_QKV, M_UNIT = 0, 1, 25
M_Z = M_UNIT + 48
M_MERGE = M_Z + 8
M_OUT = M_MERGE + 32
M_MLP = M_OUT + 16
M_PART = 32
N_DOWN, M_DOWN = N_MLP + 32, M_MLP + KT

B_P, B_X, B_XT, B_S, B_R, B_I = 2, 3, 4, 5, 6, 7


def total(static, loops):
    value = static
    for index, stride in loops:
        value = index * stride + value
    return value


def uses(static, loops, ring):
    assert all(stride % ring == 0 for _, stride in loops)
    return total(static // ring, [(index, stride // ring) for index, stride in loops])


class Chain:

    def __init__(self, engine, sem):
        self.engine, self.sem, self.base, self.loops, self.n = engine, sem, 0, [], 0

    def then(self, instruction):
        instruction.then_inc(self.sem, 1)
        self.n += 1
        self.engine.wait_ge(self.sem, total(self.base + self.n, self.loops))

    def mark(self, instruction):
        instruction.then_inc(self.sem, 1)
        self.n += 1

    @contextmanager
    def loop(self, count, per):
        with self.engine.Fori(0, count) as i:
            outer, start = self.loops, self.base + self.n
            self.base, self.n, self.loops = start, 0, [*outer, (i, per)]
            yield i
            links = self.base + self.n - start
            assert links == per, f"links in the loop: {links}"
        self.base, self.loops, self.n = start + count * per, outer, 0


def hybrid_layer(nc, x, attn_norm, w_in, gdn_conv_w, gdn_a_log, gdn_dt_bias, gdn_norm,
                 lru_conv_w, lru_conv_b, lru_w_a, lru_b_a, lru_w_x, lru_b_x, lru_lambda,
                 w_branch_gdn, w_branch_lru, w_out, mlp_norm, w_up, w_down, final_norm, out):
    ctx = ExitStack()
    with ctx:
        def sb(name, shape, dt=F32, where=ctx):
            return where.enter_context(nc.sbuf_tensor(name, shape, dt))

        def sem(name):
            return ctx.enter_context(nc.semaphore(name))

        w_raw = sb("w_raw", [P, RAW, PIECE])
        w_hi = sb("w_hi", [P, SPLIT, PIECE], F32R)
        w_lo = sb("w_lo", [P, SPLIT, PIECE], F32R)
        act_hi = sb("act_hi", [P, KT * T], F32R)
        act_lo = sb("act_lo", [P, KT * T], F32R)
        ident = sb("ident", [P, P])
        ones = sb("ones", [P, P])
        par = sb("par", [P, ROWS_A])
        conv_par = sb("conv_par", [P, ROWS_B])
        half_ba = sb("half_ba", [P, HEADS])
        half_bx = sb("half_bx", [P, HEADS])
        half_gn = sb("half_gn", [P, 1])
        nsp2 = sb("nsp2", [P, HEADS])
        eps = sb("eps", [P, 1])
        eps4 = sb("eps4", [P, 1])
        sq = sb("sq", [P, T])
        acc = sb("acc", [P, T])
        rstd = sb("rstd", [P, T])
        work = sb("work", [P, 2, T])

        with ExitStack() as first:
            x_tok = [sb(f"x_tok{t}", [P, D], where=first) for t in range(TT)]
            rows_a = sb("rows_a", [ROWS_A, P], where=first)
            rows_b = sb("rows_b", [ROWS_B, P], where=first)
            ss_x = sb("ss_x", [P, TT], where=first)
            rs_x = sb("rs_x", [P, TT], where=first)
            lam = sb("lam", [P, 6, HEADS], where=first)
        with ExitStack() as second:
            o_all = sb("o_all", [P, HEADS * T], where=second)
            lru_all = sb("lru_all", [P, HEADS * T], where=second)
            causal = sb("causal", [P, P], where=second)
            level = sb("level", [P, len(LEVELS), P], where=second)
            with ExitStack() as projecting:
                xpad_t = [sb(f"xpad_t{k}", [P, CONV - 1 + T], where=projecting) for k in range(2)]
                y_t = [sb(f"y_t{k}", [P, T], where=projecting) for k in range(2)]
                th_t = [sb(f"th_t{k}", [P, T], where=projecting) for k in range(2)]
                s_t = [sb(f"s_t{k}", [P, T], where=projecting) for k in range(6)]
                sq_t = [sb(f"sq_t{k}", [P, T], where=projecting) for k in range(4)]
                rs_t = sb("rs_t", [P, 4 * T], where=projecting)
                ab = sb("ab", [2 * HEADS, 10, T], where=projecting)
            with ExitStack() as units:
                gb_tok = sb("gb_tok", [P, 2, TT, 2 * HEADS], where=units)
                ks, qs, vs, g_bc, b_bc = [sb(n, [P, GH, P], where=units)
                                          for n in ("ks", "qs", "vs", "g_bc", "b_bc")]
                sc = sb("sc", [P, 8, GH], where=units)
                decay, e_g, attn, lt, xs, xts, prod, qd, kbg, kd, vb, nw, vnew, state = [
                    sb(n, [P, GH, P], where=units)
                    for n in ("decay", "e_g", "attn", "lt", "xs", "xts", "prod", "qd", "kbg", "kd",
                              "vb", "nw", "vnew", "state")]
                ltm = sb("ltm", [P, 2, GH, P], where=units)
                xpad = sb("xpad", [P, CONV - 1 + T], where=units)
                xc, thr, thi, tla, ysb, gel = [sb(n, [P, T], where=units)
                                               for n in ("xc", "thr", "thi", "tla", "ysb", "gel")]
                w_ga = sb("w_ga", [P, P], where=units)
                w_gx = sb("w_gx", [P, P], where=units)
                gate_out = sb("gate_out", [P, 2, T], where=units)
        with ExitStack() as third:
            sb("under_o_lru", [P, 2 * HEADS * T], where=third)
            o_hi = sb("o_hi", [P, HEADS * T], F32R, where=third)
            o_lo = sb("o_lo", [P, HEADS * T], F32R, where=third)
            lru_hi = sb("lru_hi", [P, HEADS * T], F32R, where=third)
            lru_lo = sb("lru_lo", [P, HEADS * T], F32R, where=third)
        with ExitStack() as merging:
            gate_in = sb("gate_in", [P, 2, 2, T], where=merging)
            mix = sb("mix", [P, 3, T], where=merging)
        with ExitStack() as fourth:
            x1 = sb("x1", [P, KT * T], where=fourth)
            with ExitStack() as adding:
                x_in = sb("x_in", [P, 2, TT, P], where=adding)
            u_hi = sb("u_hi", [P, KT * T], F32R, where=fourth)
            u_lo = sb("u_lo", [P, KT * T], F32R, where=fourth)

        ps = ctx.enter_context(nc.psum_tensor("ps", [P, 8, T], F32))

        qkv_dram = nc.dram_tensor("qkv_scratch", (3 * HEADS * P, T), F32, kind="Internal").ap()
        gb_dram = nc.dram_tensor("gb_scratch", (4 * HEADS, T), F32, kind="Internal").ap()
        gate_dram = nc.dram_tensor("gate_scratch", (2 * KT * P, T), F32, kind="Internal").ap()
        qkv_view = qkv_dram.rearrange("(r d) t -> d r t", d=P)

        w_loaded = [sem(f"w_loaded{s}") for s in range(RAW)]
        w_hi_ready = sem("w_hi_ready")
        w_split = [sem(f"w_split{s}") for s in range(RAW)]
        piece_done = [sem(f"piece_done{s}") for s in range(SPLIT)]
        bank_free = [sem(f"bank_free{b}") for b in range(2)]
        const_ready = sem("const_ready")
        masks_ready = sem("masks_ready")
        par_loaded = sem("par_loaded")
        par_t_ready = sem("par_t_ready")
        par_ready = sem("par_ready")
        ab_zero, ab_loaded = sem("ab_zero"), sem("ab_loaded")
        x_loaded = [sem(f"x_loaded{t}") for t in range(TT)]
        x_ss, x_ms = sem("x_ss"), sem("x_ms")
        x_rs, x_scaled = sem("x_rs"), sem("x_scaled")
        xt_done = sem("xt_done")
        act_hi_ready = sem("act_hi_ready")
        act_ready = sem("act_ready")
        act_chain, dve_chain, pool_chain = sem("act_chain"), sem("dve_chain"), sem("pool_chain")
        lam_act, lam_dve = sem("lam_act"), sem("lam_dve")
        ab_act, ab_dve = sem("ab_act"), sem("ab_dve")
        ab_t, ab_tok, gb_stored = sem("ab_t"), sem("ab_tok"), sem("gb_stored")
        pad_zero = sem("pad_zero")
        y_ready, th_ready = sem("y_ready"), sem("th_ready")
        s_ready, sq_ready = sem("s_ready"), sem("sq_ready")
        ss_ready, rs_ready = sem("ss_ready"), sem("rs_ready")
        qkv_ready, qkv_dma = sem("qkv_ready"), sem("qkv_dma")
        qkv_stored = sem("qkv_stored")
        unit_in, unit_free = sem("unit_in"), sem("unit_free")
        diff_ready, exp_ready = sem("diff_ready"), sem("exp_ready")
        heads_done, x1_done = sem("heads_done"), sem("x1_done")
        xt_start, x_copied, kv_ready = sem("xt_start"), sem("x_copied"), sem("kv_ready")
        ltm_ready, p_done, p_copied = sem("ltm_ready"), sem("p_done"), sem("p_copied")
        xx_done, x_ready = sem("xx_done"), sem("x_ready")
        w_done, nw_ready = sem("w_done"), sem("nw_ready")
        vnew_done, vnew_ready = sem("vnew_done"), sem("vnew_ready")
        o_done, state_done = sem("o_done"), sem("state_done")
        state_ready = sem("state_ready")
        o_copied, osq_ready, oss_done = sem("o_copied"), sem("osq_ready"), sem("oss_done")
        ors_ready = sem("ors_ready")
        lru_w_in = sem("lru_w_in")
        xc_ready, lgate_done = sem("xc_ready"), sem("lgate_done")
        lth_ready, tla_ready, rt_ready = sem("lth_ready"), sem("tla_ready"), sem("rt_ready")
        ysb_ready, gin_ready, gth_ready = sem("ysb_ready"), sem("gin_ready"), sem("gth_ready")
        lru_ready = sem("lru_ready")
        gate_dma, gate_free = sem("gate_dma"), [sem(f"gate_free{k}") for k in range(2)]
        z_th, z_mul, z_hi, o_ready = sem("z_th"), sem("z_mul"), sem("z_hi"), sem("o_ready")
        lru_hi_ready, lru_split = sem("lru_hi_ready"), sem("lru_split")
        gate_loaded = [sem(f"gate_loaded{k}") for k in range(2)]
        mix_ready = sem("mix_ready")
        xin_loaded = [sem(f"xin_loaded{k}") for k in range(2)]
        xin_done, xin_copied = sem("xin_done"), sem("xin_copied")
        sq1_ready, acc_done, nss_done = sem("sq1_ready"), sem("acc_done"), sem("nss_done")
        nroot_ready, h2_scaled = sem("nroot_ready"), sem("h2_scaled")
        u_sq, u_hi_ready, u_ready = sem("u_sq"), sem("u_hi_ready"), sem("u_ready")
        y_scaled, y_done, y_copied, y_dma = sem("y_scaled"), sem("y_done"), sem("y_copied"), sem("y_dma")

        block = ctx.enter_context(nc.Block())

        def heads4(tile2d, row0, tok0):
            return tile2d.rearrange("p (h t) -> p h t", t=T)[:, ds(row0, GH), ds(tok0, P)]

        def tile_wait(engine, piece, loops):
            engine.wait_ge(piece_done[piece % SPLIT], uses(piece, loops, SPLIT) + 2)

        def read_wait(engine, tile, loops):
            engine.wait_ge(bank_free[tile % 2], uses(tile, loops, 2) + 2)

        def per_head(column4):
            return column4.unsqueeze(2).to_broadcast([P, GH, P])

        def all_heads(mask):
            return mask.unsqueeze(1).to_broadcast([P, GH, P])

        def bank4(b):
            return ps[:, b, :].rearrange("p (h t) -> p h t", h=GH)

        @block.sync
        def _(sp):
            def rows(dst, r0, n, src):
                sp.dma_start(dst[r0:r0 + n, :], src).then_inc(par_loaded, 16)

            for t in range(TT):
                sp.dma_start(x_tok[t][:, :], x[0, t * P:(t + 1) * P, :]).then_inc(x_loaded[t], 16)
            rows(rows_a, R_ATTN, KT, attn_norm.rearrange("o (k p) -> (o k) p", p=P))
            rows(rows_a, R_MLP, KT, mlp_norm.rearrange("o (k p) -> (o k) p", p=P))
            rows(rows_a, R_FIN, KT, final_norm.rearrange("(k p) -> k p", p=P))
            rows(rows_a, R_LCW, CONV * HEADS, lru_conv_w.rearrange("o j (k p) -> (o j k) p", p=P))
            for r0, src in ((R_LCB, lru_conv_b), (R_BA, lru_b_a), (R_BX, lru_b_x), (R_LAM, lru_lambda)):
                rows(rows_a, r0, HEADS, src.rearrange("o (k p) -> (o k) p", p=P))
            rows(rows_a, R_GN, 1, gdn_norm)
            rows(rows_b, 0, ROWS_B, gdn_conv_w.rearrange("o j (k p) -> (o j k) p", p=P))

            def load(static, loops, weight, k0, col):
                slot = static % RAW
                sp.wait_ge(w_split[slot], uses(static, loops, RAW) + 1)
                src = weight.rearrange("(k p) n -> p k n", p=P)[:, ds(k0, KC), ds(col, P)]
                sp.dma_start(w_raw[:, slot, :].rearrange("p (k n) -> p k n", k=KC), src)\
                  .then_inc(w_loaded[slot], 16)

            for j in range(2):
                load(N_AB + j, [], w_in[0], j * KC, COL_AB)
            sp.wait_ge(ab_zero, 1)
            sp.dma_start(ab[0:HEADS, 9, 0:1], gdn_a_log.rearrange("o h -> h o")).then_inc(ab_loaded, 16)
            sp.dma_start(ab[0:HEADS, 9, 1:2], gdn_dt_bias.rearrange("o h -> h o")).then_inc(ab_loaded, 16)
            sp.wait_ge(x_ss, TT)
            with sp.Fori(0, HEADS // 2) as i:
                for j in range(12):
                    t = j // 2
                    col = (COL_V + (t - 4) * P) if t >= 4 else (COL_Q, COL_K)[t % 2] + t // 2 * P
                    load(N_QKV + j, [(i, 12)], w_in[0], j % 2 * KC, i * (2 * P) + col)
            with sp.Fori(0, GROUPS) as g:
                with sp.Fori(0, TT) as c:
                    for j in range(12):
                        t = j // 2
                        if t < 2:
                            col = c * P + (g * (TT * P) + (COL_XB, COL_YB)[t])
                        else:
                            col = c * (4 * P) + (g * (TT * 4 * P) + (COL_GATE + (t - 2) * P))
                        load(N_UNIT + j, [(g, 48), (c, 12)], w_in[0], j % 2 * KC, col)
            with sp.Fori(0, HEADS // 2) as i:
                for j in range(4):
                    load(N_Z + j, [(i, 4)], w_in[0], j % 2 * KC, i * (2 * P) + (COL_Z + j // 2 * P))
            with sp.Fori(0, KT // 2) as i:
                for j in range(4):
                    load(N_MERGE + j, [(i, 4)], (w_branch_lru, w_branch_gdn)[j % 2][0], 0,
                         i * (2 * P) + j // 2 * P)
            with sp.Fori(0, KT // 2) as i:
                for j in range(4):
                    load(N_OUT + j, [(i, 4)], w_out[0], j % 2 * KC, i * (2 * P) + j // 2 * P)
            with sp.Fori(0, FF_PARTS) as part:
                with sp.Fori(0, KT // 2) as i:
                    for j in range(4):
                        load(N_MLP + j, [(part, N_PART), (i, 4)], w_up[0], j % 2 * KC,
                             i * (2 * P) + (part * D + j // 2 * P))
                with sp.Fori(0, KT // 2) as i:
                    for j in range(4):
                        load(N_DOWN + j, [(part, N_PART), (i, 4)], w_down[0],
                             part * KT + j % 2 * KC, i * (2 * P) + j // 2 * P)

        @block.gpsimd
        def _(pool):
            pool_count = Chain(pool, pool_chain)
            nc.gpsimd.memset(ones[:, :], 1.0).then_inc(const_ready, 1)
            pool_count.then(nc.gpsimd.memset(ident[:, :], 0.0))
            nc.gpsimd.affine_select(out=ident[:, :], in_=ident[:, :], compare_op=ALU.not_equal, fill=1.0,
                                    base=0, pattern=[[-1, P]], channel_multiplier=1).then_inc(const_ready, 1)
            pool.wait_ge(xt_done, KT)
            pool.wait_ge(par_t_ready, 1)
            pool.wait_ge(lam_dve, 2)
            pool_count.mark(nc.gpsimd.memset(causal[:, :], 1.0))
            pool_count.then(nc.gpsimd.memset(level[:, :, :], 0.0))
            for n, s in enumerate(LEVELS):
                later = level[:, n, :].rearrange("p (b h r) -> p b h r", h=2, r=s)[:, :, 1, :]
                pool_count.then(nc.gpsimd.memset(later, 1.0))
                pool_count.then(nc.gpsimd.affine_select(
                    out=later, in_=later, compare_op=ALU.is_ge, fill=0.0, base=0,
                    pattern=[[-2 * s, P // (2 * s)], [0, s]], channel_multiplier=1))
                pool_count.then(nc.gpsimd.affine_select(
                    out=later, in_=later, compare_op=ALU.is_ge, fill=0.0, base=s - 1,
                    pattern=[[2 * s, P // (2 * s)], [0, s]], channel_multiplier=-1))
            nc.gpsimd.affine_select(out=causal[:, :], in_=causal[:, :], compare_op=ALU.is_ge, fill=0.0,
                                    base=0, pattern=[[1, P]], channel_multiplier=-1).then_inc(masks_ready, 1)

            pool.wait_ge(ab_dve, 3)
            pool.dma_start(gb_dram[0:2 * HEADS, :], ab[:, 7, :]).then_inc(gb_stored, 16)
            pool.dma_start(gb_dram[2 * HEADS:4 * HEADS, :], ab[:, 8, :]).then_inc(gb_stored, 16)

            with pool.Fori(0, HEADS // 2) as i:
                for n, t in enumerate((4, 0, 1, 2, 3, 5)):
                    kind, head = (2, t - 4) if t >= 4 else (t % 2, t // 2)
                    pool.wait_ge(qkv_ready, total(n + 1, [(i, 6)]))
                    pool.dma_start(qkv_dram[ds(i * (2 * P) + (kind * HEADS + head) * P, P), :],
                                   s_t[t][:, :]).then_inc(qkv_dma, 16)
                pool.wait_ge(qkv_dma, total(96, [(i, 96)]))
                pool.sem_inc(qkv_stored, 1)

            pool.wait_ge(gb_stored, 32)
            pool.wait_ge(ab_tok, 1)
            pool.wait_ge(qkv_stored, 1 + HEADS // 2)
            with pool.Fori(0, GROUPS) as g:
                with pool.Fori(0, TT) as c:
                    unit = [(g, TT), (c, 1)]
                    pool.wait_ge(unit_free, total(1, unit))
                    for dst, kind in ((ks, 1), (qs, 0), (vs, 2)):
                        pool.dma_start(dst[:, :, :], qkv_view[:, ds(g * GH + kind * HEADS, GH), ds(c * P, P)])\
                            .then_inc(unit_in, 16)
                    for dst, row in ((g_bc, 0), (b_bc, 3 * HEADS)):
                        pool.dma_start(dst[:, :, :], gb_dram[ds(g * GH + row, GH), ds(c * P, P)]
                                       .partition_broadcast(P)).then_inc(unit_in, 16)
                    pool.wait_ge(lgate_done, total(1, unit))
                    for dst, src in ((w_ga, lru_w_a), (w_gx, lru_w_x)):
                        pool.dma_start(dst[:, :], src[0].rearrange("n i j -> i n j")
                                       [:, ds(g * TT + c, 1), :].rearrange("i o j -> i (o j)"))\
                            .then_inc(lru_w_in, 16)
                    for k in range(4):
                        read_wait(pool, M_UNIT + 2 + k, [(g, 24), (c, 6)])
                        pool.dma_start(gate_dram[ds(g * (TT * 4 * P) + (c * (4 * P) + k * P), P), :],
                                       gate_out[:, k % 2, :]).then_inc(gate_dma, 16)
                        pool.wait_ge(gate_dma, total(16 * (k + 1), [(g, 64 * TT), (c, 64)]))
                        pool.sem_inc(gate_free[k % 2], 1)

            pool.wait_ge(lru_split, HEADS)
            pool.wait_ge(o_ready, HEADS)
            with pool.Fori(0, KT // 2) as i:
                for k in range(2):
                    pool.wait_ge(mix_ready, total(k + 1, [(i, 2)]))
                    for n in range(2):
                        pool.dma_start(gate_in[:, k, n, :], gate_dram[ds(i * (2 * P) + (n * KT + k) * P, P), :])\
                            .then_inc(gate_loaded[k], 16)
            pool.wait_ge(act_ready, 2 * KT)
            with pool.Fori(0, KT // 2) as i:
                for k in range(2):
                    pool.wait_ge(xin_done, total(k + 1, [(i, 2)]))
                    pool.dma_start(x_in[:, k, :, :], x[0].rearrange("(t p) n -> p t n", p=P)
                                   [:, :, ds(i * (2 * P) + k * P, P)]).then_inc(xin_loaded[k], 16)

        @block.tensor
        def _(pe):
            for s in piece_done:
                pe.sem_inc(s, 1)
            pe.sem_inc(lgate_done, 1)
            pe.sem_inc(xin_done, 2)

            def half(static, loops, part, a_hi, a_lo, k0, tile, mloops, first, last):
                raw, slot, bank = static % RAW, static % SPLIT, tile % 2
                if part == 0:
                    pe.wait_ge(w_split[raw], uses(static, loops, RAW) + 2)
                    if first:
                        pe.wait_ge(bank_free[bank], uses(tile, mloops, 2) + 1)
                for kk in range(4 * part, 4 * part + 4):
                    cols, w = slice((k0 + kk) * T, (k0 + kk + 1) * T), slice(kk * P, (kk + 1) * P)
                    for n, (wt, a) in enumerate(((w_hi, a_hi), (w_lo, a_hi), (w_hi, a_lo))):
                        mm = nc.tensor.matmul(ps[:, bank, :], wt[:, slot, w], a[:, cols],
                                              start=first and kk == 0 and n == 0,
                                              stop=last and kk == KC - 1 and n == 2)
                if part == 1:
                    mm.then_inc(piece_done[slot], 1)

            def piece(static, loops, a_hi, a_lo, k0, tile, mloops, first=None, last=None, between=()):
                first = k0 == 0 if first is None else first
                last = k0 == KC if last is None else last
                for part in range(2):
                    half(static, loops, part, a_hi, a_lo, k0, tile, mloops, first, last)
                    if part < len(between) and between[part]:
                        between[part]()

            pe.wait_ge(const_ready, 2)
            pe.wait_ge(par_loaded, 16 * 10)
            nc.tensor.transpose(ps[:, 6, 0:ROWS_A], rows_a[:, :], ident[0:ROWS_A, 0:ROWS_A])
            nc.tensor.transpose(ps[:, 6, P:P + ROWS_B], rows_b[:, :], ident[0:ROWS_B, 0:ROWS_B])\
                .then_inc(par_t_ready, 1)
            pe.wait_ge(x_scaled, TT)
            for k in range(KT):
                if k >= 4:
                    pe.wait_ge(act_ready, k - 3)
                for t in range(TT):
                    tr = nc.tensor.transpose(ps[:, 2 + k % 4, t * P:(t + 1) * P],
                                             x_tok[t][:, k * P:(k + 1) * P], ident[:, :])
                tr.then_inc(xt_done, 1)
            for j in range(2):
                pe.wait_ge(act_ready, 8 * j + 8)
                piece(N_AB + j, [], act_hi, act_lo, j * KC, M_AB, [])

            def ab_columns():
                pe.wait_ge(ab_dve, 3)
                for n in range(2):
                    for c in range(TT):
                        mm = nc.tensor.matmul(ps[:, 7, (n * TT + c) * 16:(n * TT + c + 1) * 16],
                                              ab[:, 7 + n, c * P:(c + 1) * P], ident[0:16, 0:16],
                                              start=True, stop=True)
                mm.then_inc(ab_t, 1)

            with pe.Fori(0, HEADS // 2) as i:
                def sum_squares(t):
                    pe.wait_ge(sq_ready, total(t + 1, [(i, 4)]))
                    nc.tensor.matmul(ps[:, 2 + t, :], ones[:, :], sq_t[t][:, :], start=True, stop=True)\
                        .then_inc(ss_ready, 1)

                for j in range(12):
                    between = [lambda t=(j - 4) // 2: sum_squares(t)] if j in (4, 6, 8, 10) else ()
                    piece(N_QKV + j, [(i, 12)], act_hi, act_lo, j % 2 * KC, M_QKV + j // 2, [(i, 6)],
                          between=between)
            ab_columns()

            with pe.Fori(0, GROUPS) as g:
                with pe.Fori(0, TT) as c:
                    unit, unit6 = [(g, TT), (c, 1)], [(g, 6 * TT), (c, 6)]

                    def heads(out_bank, lhs, rhs):
                        for h in range(GH):
                            mm = nc.tensor.matmul(bank4(out_bank)[:, h, :], lhs[:, h, :], rhs[:, h, :],
                                                  start=True, stop=True)
                        return mm

                    def step_heads():
                        pe.wait_ge(unit_in, total(80, [(g, 80 * TT), (c, 80)]))
                        pe.wait_ge(state_ready, total(1, unit))
                        pe.wait_ge(ors_ready, total(1, unit))
                        for h in range(GH):
                            nc.tensor.transpose(bank4(B_X)[:, h, :], ks[:, h, :], ident[:, :])
                        for h in range(GH):
                            nc.tensor.transpose(bank4(B_XT)[:, h, :], vs[:, h, :], ident[:, :])
                        heads(B_P, ks, ks)
                        heads(B_S, ks, qs).then_inc(heads_done, 1)

                    def step_first_x():
                        pe.wait_ge(kv_ready, total(1, unit))
                        for h in range(GH):
                            tr = nc.tensor.transpose(bank4(B_X)[:, h, :], xts[:, h, :], ident[:, :])
                        tr.then_inc(x1_done, 1)

                    def step_p(n):
                        pe.wait_ge(ltm_ready, total(n + 1, unit6))
                        if n == 0:
                            pe.wait_ge(x_copied, total(1, unit))
                        else:
                            pe.wait_ge(x_ready, total(n, unit6))
                        heads(B_P, ltm[:, n % 2], xs).then_inc(p_done, 1)

                    def step_x(n):
                        pe.wait_ge(p_copied, total(n + 1, unit6))
                        if n < 5:
                            heads(B_X, xts, prod)
                        heads(B_XT, prod, xts).then_inc(xx_done, 1)

                    def step_w():
                        pe.wait_ge(x_ready, total(6, unit6))
                        heads(B_P, kbg, xts).then_inc(w_done, 1)

                    def step_v():
                        pe.wait_ge(nw_ready, total(1, unit))
                        for h in range(GH):
                            nc.tensor.matmul(bank4(B_X)[:, h, :], xts[:, h, :], vb[:, h, :], start=True, stop=False)
                            mm = nc.tensor.matmul(bank4(B_X)[:, h, :], nw[:, h, :], state[:, h, :],
                                                  start=False, stop=True)
                        mm.then_inc(vnew_done, 1)

                    def step_o():
                        pe.wait_ge(vnew_ready, total(1, unit))
                        for h in range(GH):
                            nc.tensor.matmul(bank4(B_XT)[:, h, :], state[:, h, :], qd[:, h, :], start=True, stop=False)
                            mm = nc.tensor.matmul(bank4(B_XT)[:, h, :], vnew[:, h, :], attn[:, h, :],
                                                  start=False, stop=True)
                        mm.then_inc(o_done, 1)
                        heads(B_S, kd, vnew).then_inc(state_done, 1)

                    def step_norm():
                        pe.wait_ge(osq_ready, total(1, unit))
                        nc.tensor.matmul(ps[:, B_P, :], ones[:, :], sq[:, :], start=True, stop=True)\
                            .then_inc(oss_done, 1)

                    def step_lru():
                        pe.wait_ge(xc_ready, total(1, unit))
                        pe.wait_ge(lru_w_in, total(32, [(g, 32 * TT), (c, 32)]))
                        nc.tensor.matmul(ps[:, B_R, :], w_ga[:, :], xc[:, :], start=True, stop=True)
                        nc.tensor.matmul(ps[:, B_I, :], w_gx[:, :], xc[:, :], start=True, stop=True)\
                            .then_inc(lgate_done, 1)

                    steps = {3: step_heads, 6: step_first_x, 19: step_w, 20: step_v, 21: step_o,
                             22: step_norm}
                    for n in range(6):
                        steps[7 + 2 * n] = lambda n=n: step_p(n)
                        if 8 + 2 * n == 10:
                            steps[10] = lambda n=n: (step_x(n), step_lru())
                        else:
                            steps[8 + 2 * n] = lambda n=n: step_x(n)
                    for j in range(12):
                        piece(N_UNIT + j, [(g, 48), (c, 12)], act_hi, act_lo, j % 2 * KC,
                              M_UNIT + j // 2, [(g, 24), (c, 6)], between=(steps.get(2 * j), steps.get(2 * j + 1)))

            with pe.Fori(0, HEADS // 2) as i:
                for j in range(4):
                    piece(N_Z + j, [(i, 4)], act_hi, act_lo, j % 2 * KC, M_Z + j // 2, [(i, 2)])

            pe.wait_ge(lru_split, HEADS)
            with pe.Fori(0, KT // 2) as i:
                for j in range(4):
                    if j % 2 == 1:
                        pe.wait_ge(o_ready, HEADS)
                    a_hi, a_lo = ((lru_hi, lru_lo), (o_hi, o_lo))[j % 2]
                    piece(N_MERGE + j, [(i, 4)], a_hi, a_lo, 0, M_MERGE + j, [(i, 4)], True, True)

            with pe.Fori(0, KT // 2) as i:
                for j in range(4):
                    if j % 2 == 0:
                        k = j // 2
                        pe.wait_ge(xin_loaded[k], total(16, [(i, 16)]))
                        pe.wait_ge(xin_copied, total(k + 1, [(i, 2)]))
                        for t in range(TT):
                            tr = nc.tensor.transpose(ps[:, 2 + k, t * P:(t + 1) * P], x_in[:, k, t, :], ident[:, :])
                        tr.then_inc(xin_done, 1)
                    pe.wait_ge(act_ready, KT + 8 + 8 * (j % 2))
                    piece(N_OUT + j, [(i, 4)], act_hi, act_lo, j % 2 * KC, M_OUT + j // 2, [(i, 2)])

            def norm_sum(n):
                pe.wait_ge(acc_done, n)
                nc.tensor.matmul(ps[:, 4, :], ones[:, :], acc[:, :], start=True, stop=True).then_inc(nss_done, 1)

            norm_sum(KT)
            with pe.Fori(0, FF_PARTS) as part:
                with pe.Fori(0, KT // 2) as i:
                    for j in range(4):
                        pe.wait_ge(act_ready, 2 * KT + 8 + 8 * (j % 2))
                        piece(N_MLP + j, [(part, N_PART), (i, 4)], act_hi, act_lo, j % 2 * KC,
                              M_MLP + j // 2, [(part, M_PART), (i, 2)])
                with pe.Fori(0, KT // 2) as i:
                    for j in range(4):
                        pe.wait_ge(u_ready, total(8 + 8 * (j % 2), [(part, KT)]))
                        piece(N_DOWN + j, [(part, N_PART), (i, 4)], u_hi, u_lo, j % 2 * KC,
                              M_DOWN + j // 2, [(part, M_PART), (i, 2)])
            norm_sum(2 * KT)
            for k in range(KT):
                pe.wait_ge(y_scaled, k + 1)
                if k >= 4:
                    pe.wait_ge(y_copied, k - 3)
                for t in range(TT):
                    tr = nc.tensor.transpose(ps[:, 2 + k % 4, t * P:(t + 1) * P], work[:, k % 2, t * P:(t + 1) * P],
                                             ident[:, :])
                tr.then_inc(y_done, 1)

        @block.scalar
        def _(act):
            act.sem_inc(ors_ready, 1)
            act.sem_inc(xin_copied, 1)
            run = nc.scalar.activation

            def split(static, loops):
                raw, slot = static % RAW, static % SPLIT
                act.wait_ge(w_loaded[raw], uses(static, loops, RAW) * 16 + 16)
                act.wait_ge(piece_done[slot], uses(static, loops, SPLIT) + 1)
                run(w_hi[:, slot, :], w_raw[:, raw, :], ACT.Copy).then_inc(w_hi_ready, 1)

            for t in range(TT):
                act.wait_ge(x_loaded[t], 16)
                if t:
                    act.wait_ge(x_ss, t)
                run(w_raw[:, 2:4, :].rearrange("p a b -> p (a b)"), x_tok[t][:, :], ACT.Square,
                    accum_out=ss_x[:, t:t + 1]).then_inc(x_ss, 1)
            act.wait_ge(par_t_ready, 1)
            run(par[:, :], ps[:, 6, 0:ROWS_A], ACT.Copy).then_inc(par_ready, 1)
            run(conv_par[:, :], ps[:, 6, P:P + ROWS_B], ACT.Copy).then_inc(par_ready, 1)
            act.wait_ge(x_ms, 1)
            run(rs_x[:, :], rs_x[:, :], ACT.Sqrt).then_inc(x_rs, 1)
            act.wait_ge(par_ready, 2)
            for k in range(KT):
                act.wait_ge(xt_done, k + 1)
                run(act_hi[:, k * T:(k + 1) * T], ps[:, 2 + k % 4, :], ACT.Copy,
                    scale=par[:, R_ATTN + k:R_ATTN + k + 1]).then_inc(act_hi_ready, 1)
                if k in (3, 7):
                    split(k // 4, [])
            run(lam[:, 0, :], par[:, R_LAM:R_LAM + HEADS], ACT.Abs).then_inc(lam_act, 1)
            act.wait_ge(lam_act, 1)
            run(lam[:, 1, :], lam[:, 0, :], ACT.Exp, scale=-1.0).then_inc(lam_act, 1)
            act.wait_ge(lam_dve, 1)
            run(lam[:, 3, :], lam[:, 2, :], ACT.Ln).then_inc(lam_act, 1)

            tile_wait(act, 1, [])
            run(ab[:, 0, :], ps[0:2 * HEADS, 0, :], ACT.Copy).then_inc(bank_free[0], 1)
            split(2, [])
            read_wait(act, M_AB, [])
            run(ab[:, 6, :], ab[:, 0, :], ACT.Tanh, scale=0.5).then_inc(ab_act, 1)
            act.wait_ge(ab_loaded, 32)
            run(ab[:, 9, 2:3], ab[:, 9, 0:1], ACT.Exp).then_inc(ab_act, 1)
            act.wait_ge(ab_dve, 1)
            run(ab[:, 2, :], ab[:, 1, :], ACT.Abs).then_inc(ab_act, 1)
            act.wait_ge(ab_act, 3)
            run(ab[:, 3, :], ab[:, 2, :], ACT.Exp, scale=-1.0).then_inc(ab_act, 1)
            act.wait_ge(ab_dve, 2)
            run(ab[:, 5, :], ab[:, 4, :], ACT.Ln).then_inc(ab_act, 1)

            act.wait_ge(pad_zero, 2)
            with act.Fori(0, HEADS // 2) as i:
                six, four = [(i, 6)], [(i, 4)]

                def tanh_y(t):
                    act.wait_ge(y_ready, total(t + 1, six))
                    run(th_t[t % 2][:, :], y_t[t % 2][:, :], ACT.Tanh, scale=0.5).then_inc(th_ready, 1)

                for j in range(12):
                    split(N_QKV + j + 1, [(i, 12)])
                    t = j // 2
                    if j % 2 == 0:
                        if t >= 1:
                            tanh_y(t - 1)
                        continue
                    if 1 <= t <= 4:
                        act.wait_ge(s_ready, total(t, four))
                        run(sq_t[t - 1][:, :], s_t[t - 1][:, :], ACT.Square).then_inc(sq_ready, 1)
                    if t == 5:
                        act.wait_ge(ss_ready, total(4, four))
                        run(rs_t[:, :], ps[:, 2:6, :].rearrange("p b t -> p (b t)"), ACT.Sqrt,
                            bias=eps4[:, :]).then_inc(rs_ready, 1)
                    tile_wait(act, N_QKV + j, [(i, 12)])
                    run(xpad_t[t % 2][:, CONV - 1:], ps[:, (M_QKV + t) % 2, :], ACT.Copy)\
                        .then_inc(bank_free[(M_QKV + t) % 2], 1)
                tanh_y(5)

            act.wait_ge(ab_t, 1)
            act.wait_ge(qkv_stored, 1 + HEADS // 2)
            run(gb_tok[:, :, :, :].rearrange("p a c n -> p (a c n)"), ps[:, 7, 0:P], ACT.Copy).then_inc(ab_tok, 1)

            with act.Fori(0, GROUPS) as g:
                with act.Fori(0, TT) as c:
                    unit, unit2, unit6 = [(g, TT), (c, 1)], [(g, 2 * TT), (c, 2)], [(g, 6 * TT), (c, 6)]
                    pieces, block_n = [(g, 48), (c, 12)], g * TT + c

                    def gate(k):
                        tile_wait(act, N_UNIT + 5 + 2 * k, pieces)
                        act.wait_ge(gate_free[k % 2], total(k // 2 + 1, unit2))
                        run(gate_out[:, k % 2, :], ps[:, (M_UNIT + k) % 2, :], ACT.Tanh, scale=0.5)\
                            .then_inc(bank_free[(M_UNIT + k) % 2], 1)

                    for j in range(12):
                        split(N_UNIT + j + 1, pieces)
                        if j == 1:
                            act.wait_ge(diff_ready, total(1, unit))
                            run(decay[:, :, :], decay[:, :, :], ACT.Exp).then_inc(exp_ready, 1)
                            run(e_g[:, :, :], g_bc[:, :, :], ACT.Exp).then_inc(exp_ready, 1)
                            run(sc[:, 3:6, :], sc[:, 0:3, :], ACT.Exp).then_inc(exp_ready, 1)
                            tile_wait(act, N_UNIT + 1, pieces)
                            run(xpad[:, CONV - 1:], ps[:, M_UNIT % 2, :], ACT.Copy)\
                                .then_inc(bank_free[M_UNIT % 2], 1)
                        if j == 3:
                            act.wait_ge(x1_done, total(1, unit))
                            run(xs[:, :, :], bank4(B_X), ACT.Copy).then_inc(x_copied, 1)
                            tile_wait(act, N_UNIT + 3, pieces)
                            run(ysb[:, :], ps[:, (M_UNIT + 1) % 2, :], ACT.Copy).then_inc(ysb_ready, 1)
                            run(gel[:, :], ps[:, (M_UNIT + 1) % 2, :], ACT.Square)\
                                .then_inc(bank_free[(M_UNIT + 1) % 2], 1)
                        if j == 5:
                            act.wait_ge(gin_ready, total(1, unit))
                            run(gel[:, :], gel[:, :], ACT.Tanh, scale=GELU_SCALE).then_inc(gth_ready, 1)
                            act.wait_ge(lgate_done, total(2, unit))
                            run(thr[:, :], ps[:, B_R, :], ACT.Tanh, scale=0.5, bias=half_ba[:, ds(block_n, 1)])\
                                .then_inc(lth_ready, 1)
                            run(thi[:, :], ps[:, B_I, :], ACT.Tanh, scale=0.5, bias=half_bx[:, ds(block_n, 1)])\
                                .then_inc(lth_ready, 1)
                        if j == 6:
                            act.wait_ge(lth_ready, total(2, unit2))
                            run(tla[:, :], thr[:, :], ACT.Tanh, scale=nsp2[:, ds(block_n, 1)],
                                bias=nsp2[:, ds(block_n, 1)]).then_inc(tla_ready, 1)
                        if j == 11:
                            act.wait_ge(oss_done, total(1, unit))
                            run(rstd[:, :], ps[:, B_P, :], ACT.Sqrt, scale=1.0 / P, bias=eps[:, :])\
                                .then_inc(ors_ready, 1)
                        if j in (5, 7, 9, 11):
                            gate((j - 5) // 2)
                        if 3 <= j <= 8:
                            act.wait_ge(p_done, total(j - 2, unit6))
                            run(prod[:, :, :], bank4(B_P), ACT.Copy).then_inc(p_copied, 1)
                        if j == 7:
                            act.wait_ge(tla_ready, total(1, unit))
                            run(thr[:, :], tla[:, :], ACT.Sqrt, scale=-1.0).then_inc(rt_ready, 1)
                        if j == 9:
                            act.wait_ge(w_done, total(1, unit))
                            run(nw[:, :, :], bank4(B_P), ACT.Copy, scale=-1.0).then_inc(nw_ready, 1)
                        if j == 10:
                            act.wait_ge(vnew_done, total(1, unit))
                            run(vnew[:, :, :], bank4(B_X), ACT.Copy).then_inc(vnew_ready, 1)
                            act.wait_ge(o_done, total(1, unit))
                            run(prod[:, :, :], bank4(B_XT), ACT.Copy).then_inc(o_copied, 1)
                            act.wait_ge(o_copied, total(1, unit))
                            run(sq[:, :], prod[:, :, :].rearrange("p h t -> p (h t)"), ACT.Square)\
                                .then_inc(osq_ready, 1)

            for k in range(2):
                act.wait_ge(gate_free[k], 1 + 2 * GROUPS * TT)
            with act.Fori(0, HEADS // 2) as i:
                for j in range(4):
                    split(N_Z + j + 1, [(i, 4)])
                    if j % 2 == 1:
                        k = j // 2
                        at = ds(i * (2 * T) + k * T, T)
                        tile_wait(act, N_Z + j, [(i, 4)])
                        run(work[:, 0, :], ps[:, (M_Z + k) % 2, :], ACT.Tanh, scale=0.5).then_inc(z_th, 1)
                        act.wait_ge(lru_ready, HEADS)
                        run(lru_hi[:, at], lru_all[:, at], ACT.Copy).then_inc(lru_hi_ready, 1)
                        act.wait_ge(z_mul, total(k + 1, [(i, 2)]))
                        run(o_hi[:, at], work[:, 1, :], ACT.Copy, scale=half_gn[:, :]).then_inc(z_hi, 1)

            with act.Fori(0, KT // 2) as i:
                for j in range(4):
                    split(N_MERGE + j + 1, [(i, 4)])
                    if j % 2 == 1:
                        k = j // 2
                        act.wait_ge(mix_ready, total(k + 3, [(i, 2)]))
                        run(act_hi[:, ds(i * (2 * T) + k * T, T)], mix[:, 2, :], ACT.Copy, scale=0.5)\
                            .then_inc(act_hi_ready, 1)

            with act.Fori(0, KT // 2) as i:
                for j in range(4):
                    split(N_OUT + j + 1, [(i, 4)])
                    k = j // 2
                    if j % 2 == 0:
                        act.wait_ge(xin_done, total(k + 3, [(i, 2)]))
                        run(work[:, k, :], ps[:, 2 + k, :], ACT.Copy).then_inc(xin_copied, 1)
                    else:
                        read_wait(act, M_OUT + k, [(i, 2)])
                        run(sq[:, :], x1[:, ds(i * (2 * T) + k * T, T)], ACT.Square).then_inc(sq1_ready, 1)

            def root(n):
                act.wait_ge(nss_done, n)
                run(rstd[:, :], ps[:, 4, :], ACT.Sqrt, scale=1.0 / D, bias=eps[:, :]).then_inc(nroot_ready, 1)

            root(1)
            for k in range(KT):
                act.wait_ge(h2_scaled, k + 1)
                run(act_hi[:, k * T:(k + 1) * T], work[:, k % 2, :], ACT.Copy,
                    scale=par[:, R_MLP + k:R_MLP + k + 1]).then_inc(act_hi_ready, 1)

            def up(part):
                with act.Fori(0, KT // 2) as i:
                    for j in range(4):
                        split(N_MLP + j + 1, [(part, N_PART), (i, 4)])
                        if j % 2 == 1:
                            k = j // 2
                            tile_wait(act, N_MLP + j, [(part, N_PART), (i, 4)])
                            run(work[:, k, :], ps[:, (M_MLP + k) % 2, :], ACT.Relu)\
                                .then_inc(bank_free[(M_MLP + k) % 2], 1)
                            act.wait_ge(u_sq, total(k + 1, [(part, KT), (i, 2)]))
                            run(u_hi[:, ds(i * (2 * T) + k * T, T)], rstd[:, :], ACT.Copy).then_inc(u_hi_ready, 1)

            def down(part, i, last_part=False, end=False):
                for j in range(4):
                    if not (end and j == 3):
                        split(N_DOWN + j + 1, [(part, N_PART), (i, 4)])
                    if last_part and j % 2 == 1:
                        k = j // 2
                        read_wait(act, M_DOWN + k, [(part, M_PART), (i, 2)])
                        run(sq[:, :], x1[:, ds(i * (2 * T) + k * T, T)], ACT.Square).then_inc(sq1_ready, 1)

            with act.Fori(0, FF_PARTS - 1) as part:
                up(part)
                with act.Fori(0, KT // 2) as i:
                    down(part, i)
            up(FF_PARTS - 1)
            with act.Fori(0, KT // 2 - 1) as i:
                down(FF_PARTS - 1, i, last_part=True)
            down(FF_PARTS - 1, KT // 2 - 1, last_part=True, end=True)

            root(2)
            for k in range(KT):
                tile = x1[:, k * T:(k + 1) * T]
                act.wait_ge(y_done, k + 1)
                run(tile, ps[:, 2 + k % 4, :], ACT.Copy).then_inc(y_copied, 1)
                act.wait_ge(y_copied, k + 1)
                act.dma_start(out[0].rearrange("(t p) n -> p t n", p=P)[:, :, k * P:(k + 1) * P],
                              tile.rearrange("p (t n) -> p t n", t=TT)).then_inc(y_dma, 16)
            act.wait_ge(y_dma, 16 * KT)

        @block.vector
        def _(dve):
            chain = Chain(dve, dve_chain)
            for s in (*w_split, *bank_free, qkv_stored, unit_free, state_ready, *gate_free):
                dve.sem_inc(s, 1)
            dve.sem_inc(mix_ready, 2)
            tt, ts, stt = nc.vector.tensor_tensor, nc.vector.tensor_scalar, nc.vector.scalar_tensor_tensor

            def split(static, loops):
                raw, slot = static % RAW, static % SPLIT
                dve.wait_ge(w_hi_ready, total(static + 1, loops))
                tt(w_lo[:, slot, :], w_raw[:, raw, :], w_hi[:, slot, :].bitcast(F32), ALU.subtract)\
                    .then_inc(w_split[raw], 1)

            def conv(y, padded, weights, col, bias=None):
                def weight(n):
                    return weights[:, ds(col(n), 1)]
                chain.then(ts(y, padded[:, 0:T], weight(0), bias, ALU.mult, ALU.add) if bias is not None
                           else ts(y, padded[:, 0:T], weight(0), None, ALU.mult))
                for n in range(1, CONV):
                    last = stt(out=y, in0=padded[:, n:n + T], scalar=weight(n), in1=y, op0=ALU.mult, op1=ALU.add)
                    if n < CONV - 1:
                        chain.then(last)
                return last

            def log1p_rest(l, e, u, t):
                chain.then(ts(t, u, -1.0, None, ALU.add))
                chain.then(tt(t, e, t, ALU.subtract))
                chain.then(nc.vector.reciprocal(u, u))
                chain.then(tt(t, t, u, ALU.mult))
                chain.then(tt(l, l, t, ALU.add))

            nc.vector.memset(eps[:, :], RMS_EPS)
            chain.then(nc.vector.memset(eps4[:, :], 4 * L2_EPS))
            nc.vector.memset(ab[:, 9, :], 0.0).then_inc(ab_zero, 1)
            dve.wait_ge(x_ss, TT)
            chain.then(ts(rs_x[:, :], ss_x[:, :], 1.0 / D, RMS_EPS, ALU.mult, ALU.add))
            nc.vector.reciprocal(rs_x[:, :], rs_x[:, :]).then_inc(x_ms, 1)
            dve.wait_ge(x_rs, 1)
            for t in range(TT):
                ts(x_tok[t][:, :], x_tok[t][:, :], rs_x[:, t:t + 1], None, ALU.mult).then_inc(x_scaled, 1)
            for k in range(KT):
                dve.wait_ge(act_hi_ready, k + 1)
                cols = slice(k * T, (k + 1) * T)
                stt(out=act_lo[:, cols], in0=ps[:, 2 + k % 4, :], scalar=par[:, R_ATTN + k:R_ATTN + k + 1],
                    in1=act_hi[:, cols].bitcast(F32), op0=ALU.mult, op1=ALU.subtract).then_inc(act_ready, 1)
                if k in (3, 7):
                    split(k // 4, [])
            dve.wait_ge(lam_act, 2)
            ts(lam[:, 2, :], lam[:, 1, :], 1.0, None, ALU.add).then_inc(lam_dve, 1)
            dve.wait_ge(lam_act, 3)
            log1p_rest(lam[:, 3, :], lam[:, 1, :], lam[:, 2, :], lam[:, 4, :])
            chain.then(ts(lam[:, 5, :], par[:, R_LAM:R_LAM + HEADS], -1.0, 0.0, ALU.mult, ALU.max))
            chain.then(tt(lam[:, 3, :], lam[:, 3, :], lam[:, 5, :], ALU.add))
            ts(half_ba[:, :], par[:, R_BA:R_BA + HEADS], 0.5, None, ALU.mult)
            ts(half_bx[:, :], par[:, R_BX:R_BX + HEADS], 0.5, None, ALU.mult)
            ts(half_gn[:, :], par[:, R_GN:R_GN + 1], 0.5, None, ALU.mult)
            ts(nsp2[:, :], lam[:, 3, :], -2.0, None, ALU.mult).then_inc(lam_dve, 1)

            split(2, [])
            read_wait(dve, M_AB, [])
            dve.wait_ge(ab_loaded, 32)
            ts(ab[:, 1, :], ab[:, 0, :], ab[:, 9, 1:2], None, ALU.add).then_inc(ab_dve, 1)
            dve.wait_ge(ab_act, 4)
            ts(ab[:, 4, :], ab[:, 3, :], 1.0, None, ALU.add).then_inc(ab_dve, 1)
            chain.then(ts(ab[:, 1, :], ab[:, 1, :], 0.0, None, ALU.max))
            chain.then(ts(ab[:, 9, 2:3], ab[:, 9, 2:3], -1.0, None, ALU.mult))
            dve.wait_ge(ab_act, 5)
            log1p_rest(ab[:, 5, :], ab[:, 3, :], ab[:, 4, :], ab[:, 2, :])
            chain.then(tt(ab[:, 5, :], ab[:, 5, :], ab[:, 1, :], ALU.add))
            chain.then(ts(ab[:, 5, :], ab[:, 5, :], ab[:, 9, 2:3], None, ALU.mult))
            for c in range(TT):
                cols = slice(c * P, (c + 1) * P)
                nc.vector.tensor_tensor_scan(ab[:, 7, cols], ones[0:2 * HEADS, :], ab[:, 5, cols], 0.0,
                                             ALU.mult, ALU.add)
            ts(ab[:, 8, :], ab[:, 6, :], 0.5, 0.5, ALU.mult, ALU.add).then_inc(ab_dve, 1)

            for xp in xpad_t:
                nc.vector.memset(xp[:, 0:CONV - 1], 0.0).then_inc(pad_zero, 1)
            dve.wait_ge(pad_zero, 2)
            with chain.loop(HEADS // 2, 19) as i:
                six, four = [(i, 6)], [(i, 4)]

                def convolve(t):
                    kind, head = (2, t - 4) if t >= 4 else (t % 2, t // 2)
                    read_wait(dve, M_QKV + t, six)
                    conv(y_t[t % 2][:, :], xpad_t[t % 2], conv_par,
                         lambda n: i * 2 + (n * 3 * HEADS + kind * HEADS + head)).then_inc(y_ready, 1)

                def silu2(t):
                    dve.wait_ge(th_ready, total(t + 1, six))
                    return stt(out=s_t[t][:, :], in0=th_t[t % 2][:, :], scalar=1.0, in1=y_t[t % 2][:, :],
                               op0=ALU.add, op1=ALU.mult)

                for j in range(12):
                    split(N_QKV + j + 1, [(i, 12)])
                    if j % 2 == 0:
                        if j >= 2:
                            convolve(j // 2 - 1)
                        continue
                    if j == 3:
                        dve.wait_ge(qkv_stored, total(1, [(i, 1)]))
                    if 3 <= j <= 9:
                        dve.wait_ge(y_ready, total((j - 1) // 2, six))
                        silu2((j - 3) // 2).then_inc(s_ready, 1)
                    if j == 11:
                        dve.wait_ge(y_ready, total(5, six))
                        silu2(4).then_inc(qkv_ready, 1)
                        dve.wait_ge(rs_ready, total(1, [(i, 1)]))
                        chain.then(nc.vector.reciprocal(rs_t[:, :], rs_t[:, :]))
                        for t in range(4):
                            stt(out=s_t[t][:, :], in0=s_t[t][:, :], scalar=(QK, 1.0)[t % 2],
                                in1=rs_t[:, t * T:(t + 1) * T], op0=ALU.mult, op1=ALU.mult).then_inc(qkv_ready, 1)
                convolve(5)
                dve.wait_ge(y_ready, total(6, six))
                silu2(5).then_inc(qkv_ready, 1)

            dve.wait_ge(qkv_stored, 1 + HEADS // 2)
            dve.wait_ge(ab_tok, 1)
            dve.wait_ge(gb_stored, 32)
            dve.wait_ge(masks_ready, 1)
            chain.then(nc.vector.memset(xpad[:, 0:CONV - 1], 0.0))
            with chain.loop(GROUPS, 1 + TT * UNIT_LINKS) as g:
                chain.mark(nc.vector.memset(state[:, :, :], 0.0))
                with chain.loop(TT, UNIT_LINKS) as c:
                    unit, unit3, unit6 = [(g, TT), (c, 1)], [(g, 3 * TT), (c, 3)], [(g, 6 * TT), (c, 6)]
                    pieces, block_n = [(g, 48), (c, 12)], g * TT + c

                    def level_mask(n):
                        tt(ltm[:, n % 2, :, :], lt[:, :, :], all_heads(level[:, n + 1, :]), ALU.mult)\
                            .then_inc(ltm_ready, 1)

                    for j in range(12):
                        split(N_UNIT + j + 1, pieces)
                        if j == 0:
                            dve.wait_ge(unit_in, total(80, [(g, 80 * TT), (c, 80)]))
                            g_col = gb_tok[:, 0, ds(c, 1), ds(g * GH, GH)]
                            b_col = gb_tok[:, 1, ds(c, 1), ds(g * GH + HEADS, GH)]
                            nc.vector.tensor_copy(sc[:, 1:2, :], g_col)
                            ts(sc[:, 6:7, :], b_col, 0.5, None, ALU.mult)
                            chain.then(nc.vector.tensor_copy(sc[:, 2:3, :].rearrange("p o h -> p h o"),
                                                             g_bc[:, :, P - 1:P]))
                            tt(sc[:, 0, :], sc[:, 2, :], sc[:, 1, :], ALU.subtract)
                            chain.then(tt(decay[:, :, :], g_bc[:, :, :], per_head(sc[:, 1, :]), ALU.subtract))
                            ts(decay[:, :, :], decay[:, :, :], 0.0, None, ALU.min).then_inc(diff_ready, 1)
                        if j == 1:
                            dve.wait_ge(exp_ready, total(3, unit3))
                            tt(sc[:, 7, :], sc[:, 6, :], sc[:, 4, :], ALU.mult)
                            tt(qd[:, :, :], qs[:, :, :], e_g[:, :, :], ALU.mult)
                            chain.then(tt(decay[:, :, :], decay[:, :, :], all_heads(causal[:, :]), ALU.mult))
                            chain.then(tt(e_g[:, :, :], decay[:, :, :], b_bc[:, :, :], ALU.mult))
                        if j == 2:
                            dve.wait_ge(heads_done, total(1, unit))
                            tt(lt[:, :, :], bank4(B_P), e_g[:, :, :], ALU.mult).then_inc(unit_free, 1)
                            dve.wait_ge(unit_free, total(2, unit))
                            chain.then(tt(xts[:, :, :], lt[:, :, :], all_heads(level[:, 0, :]), ALU.mult))
                            tt(xts[:, :, :], all_heads(ident[:, :]), xts[:, :, :], ALU.subtract)
                            stt(out=kbg[:, :, :], in0=bank4(B_X), scalar=2.0, in1=per_head(sc[:, 7, :]),
                                op0=ALU.mult, op1=ALU.mult)
                            tt(kd[:, :, :], bank4(B_X), per_head(sc[:, 3, :]), ALU.mult)
                            tt(vb[:, :, :], bank4(B_XT), per_head(sc[:, 6, :]), ALU.mult).then_inc(kv_ready, 1)
                        if j == 3:
                            level_mask(0)
                            tt(attn[:, :, :], bank4(B_S), decay[:, :, :], ALU.mult)
                            read_wait(dve, M_UNIT, [(g, 24), (c, 6)])
                            conv(xc[:, :], xpad, par, lambda n: g * TT + (c + (R_LCW + n * HEADS)),
                                 bias=par[:, ds(g * TT + (c + R_LCB), 1)]).then_inc(xc_ready, 1)
                        if 4 <= j <= 9:
                            n = j - 4
                            if n < 5:
                                level_mask(n + 1)
                            dve.wait_ge(xx_done, total(n + 1, unit6))
                            if n < 5:
                                tt(xs[:, :, :], xs[:, :, :], bank4(B_X), ALU.subtract)
                            tt(xts[:, :, :], xts[:, :, :], bank4(B_XT), ALU.subtract).then_inc(x_ready, 1)
                        if j == 4:
                            dve.wait_ge(ysb_ready, total(1, unit))
                            read_wait(dve, M_UNIT + 1, [(g, 24), (c, 6)])
                            chain.then(ts(gel[:, :], gel[:, :], GELU_CUBIC, 1.0, ALU.mult, ALU.add))
                            tt(gel[:, :], gel[:, :], ysb[:, :], ALU.mult).then_inc(gin_ready, 1)
                        if j == 6:
                            dve.wait_ge(gth_ready, total(1, unit))
                            chain.then(stt(out=ysb[:, :], in0=gel[:, :], scalar=1.0, in1=ysb[:, :],
                                           op0=ALU.add, op1=ALU.mult))
                        if j == 7:
                            dve.wait_ge(tla_ready, total(1, unit))
                            chain.then(ts(gel[:, :], tla[:, :], -1.0, 1.0, ALU.mult, ALU.add))
                            chain.then(nc.vector.reciprocal(gel[:, :], gel[:, :]))
                            chain.then(stt(out=thi[:, :], in0=thi[:, :], scalar=1.0, in1=xc[:, :],
                                           op0=ALU.add, op1=ALU.mult))
                            chain.then(tt(thi[:, :], thi[:, :], gel[:, :], ALU.mult))
                        if j == 8:
                            dve.wait_ge(rt_ready, total(1, unit))
                            tt(thi[:, :], thi[:, :], thr[:, :], ALU.mult)
                            chain.then(stt(out=tla[:, :], in0=tla[:, :], scalar=1.0, in1=gel[:, :],
                                           op0=ALU.add, op1=ALU.mult))
                            chain.then(nc.vector.tensor_tensor_scan(gel[:, :], tla[:, :], thi[:, :], 0.0,
                                                                    ALU.mult, ALU.add))
                            stt(out=lru_all[:, ds(block_n * T, T)], in0=gel[:, :], scalar=0.5, in1=ysb[:, :],
                                op0=ALU.mult, op1=ALU.mult).then_inc(lru_ready, 1)
                        if j == 10:
                            dve.wait_ge(state_done, total(1, unit))
                            for h in range(GH):
                                last = stt(out=state[:, h, :], in0=state[:, h, :], scalar=sc[:, 5, h:h + 1],
                                           in1=bank4(B_S)[:, h, :], op0=ALU.mult, op1=ALU.add)
                            last.then_inc(state_ready, 1)
                        if j == 11:
                            dve.wait_ge(ors_ready, total(2, unit))
                            chain.then(nc.vector.reciprocal(rstd[:, :], rstd[:, :]))
                            chain.then(tt(heads4(o_all[:, :], g * GH, c * P), prod[:, :, :],
                                          rstd[:, :].rearrange("p (h t) -> p h t", h=GH), ALU.mult))

            for k in range(2):
                dve.wait_ge(gate_free[k], 1 + 2 * GROUPS * TT)
            with dve.Fori(0, HEADS // 2) as i:
                for j in range(4):
                    split(N_Z + j + 1, [(i, 4)])
                    if j % 2 == 1:
                        k = j // 2
                        at = ds(i * (2 * T) + k * T, T)
                        dve.wait_ge(z_th, total(k + 1, [(i, 2)]))
                        stt(out=work[:, 1, :], in0=work[:, 0, :], scalar=1.0, in1=ps[:, (M_Z + k) % 2, :],
                            op0=ALU.add, op1=ALU.mult).then_inc(bank_free[(M_Z + k) % 2], 1)
                        read_wait(dve, M_Z + k, [(i, 2)])
                        tt(work[:, 1, :], work[:, 1, :], o_all[:, at], ALU.mult).then_inc(z_mul, 1)
                        dve.wait_ge(lru_hi_ready, total(k + 1, [(i, 2)]))
                        tt(lru_lo[:, at], lru_all[:, at], lru_hi[:, at].bitcast(F32), ALU.subtract)\
                            .then_inc(lru_split, 1)
                        dve.wait_ge(z_hi, total(k + 1, [(i, 2)]))
                        stt(out=o_lo[:, at], in0=work[:, 1, :], scalar=half_gn[:, :],
                            in1=o_hi[:, at].bitcast(F32), op0=ALU.mult, op1=ALU.subtract).then_inc(o_ready, 1)

            with dve.Fori(0, KT // 2) as i:
                for j in range(4):
                    split(N_MERGE + j + 1, [(i, 4)])
                    k, n = j // 2, j % 2
                    dve.wait_ge(gate_loaded[k], total(32, [(i, 32)]))
                    tile_wait(dve, N_MERGE + j, [(i, 4)])
                    stt(out=mix[:, n, :], in0=gate_in[:, k, 1 - n, :], scalar=1.0, in1=ps[:, (M_MERGE + j) % 2, :],
                        op0=ALU.add, op1=ALU.mult).then_inc(bank_free[(M_MERGE + j) % 2], 1)
                    if n == 1:
                        at = ds(i * (2 * T) + k * T, T)
                        read_wait(dve, M_MERGE + j, [(i, 4)])
                        tt(mix[:, 2, :], mix[:, 0, :], mix[:, 1, :], ALU.add).then_inc(mix_ready, 1)
                        dve.wait_ge(act_hi_ready, total(KT + k + 1, [(i, 2)]))
                        stt(out=act_lo[:, at], in0=mix[:, 2, :], scalar=0.5, in1=act_hi[:, at].bitcast(F32),
                            op0=ALU.mult, op1=ALU.subtract).then_inc(act_ready, 1)

            chain.then(nc.vector.memset(acc[:, :], 0.0))
            with dve.Fori(0, KT // 2) as i:
                for j in range(4):
                    split(N_OUT + j + 1, [(i, 4)])
                    if j % 2 == 1:
                        k = j // 2
                        tile_wait(dve, N_OUT + j, [(i, 4)])
                        dve.wait_ge(xin_copied, total(k + 2, [(i, 2)]))
                        tt(x1[:, ds(i * (2 * T) + k * T, T)], work[:, k, :], ps[:, (M_OUT + k) % 2, :], ALU.add)\
                            .then_inc(bank_free[(M_OUT + k) % 2], 1)
                        dve.wait_ge(sq1_ready, total(k + 1, [(i, 2)]))
                        tt(acc[:, :], acc[:, :], sq[:, :], ALU.add).then_inc(acc_done, 1)
                        dve.wait_ge(acc_done, total(k + 1, [(i, 2)]))

            def root(n):
                dve.wait_ge(nroot_ready, n)
                chain.then(nc.vector.reciprocal(rstd[:, :], rstd[:, :]))

            root(1)

            def scale_x1(k):
                tt(work[:, k % 2, :], x1[:, k * T:(k + 1) * T], rstd[:, :], ALU.mult).then_inc(h2_scaled, 1)

            scale_x1(0)
            for k in range(KT):
                cols = slice(k * T, (k + 1) * T)
                if k + 1 < KT:
                    if k:
                        dve.wait_ge(act_ready, 2 * KT + k)
                    scale_x1(k + 1)
                dve.wait_ge(h2_scaled, k + 1)
                dve.wait_ge(act_hi_ready, 2 * KT + k + 1)
                stt(out=act_lo[:, cols], in0=work[:, k % 2, :], scalar=par[:, R_MLP + k:R_MLP + k + 1],
                    in1=act_hi[:, cols].bitcast(F32), op0=ALU.mult, op1=ALU.subtract).then_inc(act_ready, 1)

            def up(part):
                with dve.Fori(0, KT // 2) as i:
                    for j in range(4):
                        split(N_MLP + j + 1, [(part, N_PART), (i, 4)])
                        if j % 2 == 1:
                            k = j // 2
                            read_wait(dve, M_MLP + k, [(part, M_PART), (i, 2)])
                            tt(rstd[:, :], work[:, k, :], work[:, k, :], ALU.mult).then_inc(u_sq, 1)
                            at = ds(i * (2 * T) + k * T, T)
                            dve.wait_ge(u_hi_ready, total(k + 1, [(part, KT), (i, 2)]))
                            tt(u_lo[:, at], rstd[:, :], u_hi[:, at].bitcast(F32), ALU.subtract).then_inc(u_ready, 1)

            def down(part, i, last_part=False, end=False):
                for j in range(4):
                    if not (end and j == 3):
                        split(N_DOWN + j + 1, [(part, N_PART), (i, 4)])
                    if j % 2 == 1:
                        k = j // 2
                        at = ds(i * (2 * T) + k * T, T)
                        tile_wait(dve, N_DOWN + j, [(part, N_PART), (i, 4)])
                        tt(x1[:, at], x1[:, at], ps[:, (M_DOWN + k) % 2, :], ALU.add)\
                            .then_inc(bank_free[(M_DOWN + k) % 2], 1)
                        if last_part:
                            dve.wait_ge(sq1_ready, total(KT + k + 1, [(i, 2)]))
                            tt(acc[:, :], acc[:, :], sq[:, :], ALU.add).then_inc(acc_done, 1)
                            dve.wait_ge(acc_done, total(KT + k + 1, [(i, 2)]))

            with dve.Fori(0, FF_PARTS - 1) as part:
                up(part)
                with dve.Fori(0, KT // 2) as i:
                    down(part, i)
            up(FF_PARTS - 1)
            chain.then(nc.vector.memset(acc[:, :], 0.0))
            with dve.Fori(0, KT // 2 - 1) as i:
                down(FF_PARTS - 1, i, last_part=True)
            down(FF_PARTS - 1, KT // 2 - 1, last_part=True, end=True)

            root(2)
            for k in range(KT):
                if k >= 2:
                    dve.wait_ge(y_done, k - 1)
                stt(out=work[:, k % 2, :], in0=x1[:, k * T:(k + 1) * T], scalar=par[:, R_FIN + k:R_FIN + k + 1],
                    in1=rstd[:, :], op0=ALU.mult, op1=ALU.mult).then_inc(y_scaled, 1)


_INS = ['x', 'attn_norm', 'w_in', 'gdn_conv_w', 'gdn_a_log', 'gdn_dt_bias', 'gdn_norm', 'lru_conv_w',
        'lru_conv_b', 'lru_w_a', 'lru_b_a', 'lru_w_x', 'lru_b_x', 'lru_lambda', 'w_branch_gdn',
        'w_branch_lru', 'w_out', 'mlp_norm', 'w_up', 'w_down', 'final_norm']


def kernel(**inputs):
    import numpy as _np
    import concourse.bacc as _bacc
    from concourse import mybir as _mybir
    from concourse.bass_utils import run_bass_kernel_spmd as _run

    nc = _bacc.Bacc("TRN2", target_bir_lowering=False, num_devices=1)
    arrays, args = {}, []
    for name in _INS:
        a = _np.ascontiguousarray(inputs[name])
        arrays[f"in_{name}_dram"] = a
        args.append(nc.dram_tensor(f"in_{name}_dram", a.shape, _mybir.dt.from_np(a.dtype), kind="ExternalInput").ap())
    result = nc.dram_tensor("out_dram", (1, T, D), F32, kind="ExternalOutput").ap()
    hybrid_layer(nc, *args, result)
    r = _run(nc, [arrays], core_ids=[0])
    return r.results[0]["out_dram"]
```

```python
from contextlib import ExitStack, contextmanager

import concourse.bass as bass
from concourse import mybir

F32 = mybir.dt.float32
F32R = mybir.dt.float32r
ALU = mybir.AluOpType
ACT = mybir.ActivationFunctionType
ds = bass.ds

P = 128
T = 512
TT = T // P
D = 2048
KT = D // P
HEADS = 8
BW = HEADS * P
GH = 4
GROUPS = HEADS // GH
CONV = 4
FF_PARTS = 4
LEVELS = [1 << n for n in range(7)]
RMS_EPS = 1e-6
L2_EPS = 1e-6
GELU_CUBIC = 0.044715
GELU_SCALE = 0.7978845608028654
QK = P ** -0.5

COL_Q, COL_K, COL_V, COL_Z = 0, BW, 2 * BW, 3 * BW
COL_AB = 4 * BW
COL_XB = COL_AB + 2 * HEADS
COL_YB = COL_XB + BW
COL_GATE = COL_YB + BW

R_ATTN, R_MLP, R_FIN = 0, KT, 2 * KT
R_LCW = 3 * KT
R_LCB = R_LCW + CONV * HEADS
R_BA, R_BX, R_LAM = R_LCB + 8, R_LCB + 16, R_LCB + 24
R_GN = R_LCB + 32
ROWS_A = R_GN + 1
ROWS_B = CONV * 3 * HEADS

RAW, SPLIT = 4, 2
KC = 8
QUADS = KT // 4
PIECE = KC * P

N_QKV, N_UNIT = 0, 48
N_Z = N_UNIT + 96
N_MERGE = N_Z + 16
N_OUT = N_MERGE + 32
N_MLP = N_OUT + 32
N_PART = 64
UNIT_LINKS = 24
M_QKV, M_UNIT = 0, 24
M_Z = M_UNIT + 48
M_MERGE = M_Z + 8
M_OUT = M_MERGE + 32
M_MLP = M_OUT + 16
M_PART = 32
N_DOWN, M_DOWN = N_MLP + 32, M_MLP + KT

B_P, B_X, B_XT, B_S, B_R, B_I = 2, 3, 4, 5, 6, 7


def total(static, loops):
    value = static
    for index, stride in loops:
        value = index * stride + value
    return value


def uses(static, loops, ring):
    assert all(stride % ring == 0 for _, stride in loops)
    return total(static // ring, [(index, stride // ring) for index, stride in loops])


class Chain:

    def __init__(self, engine, sem):
        self.engine, self.sem, self.base, self.loops, self.n = engine, sem, 0, [], 0

    def then(self, instruction):
        instruction.then_inc(self.sem, 1)
        self.n += 1
        self.engine.wait_ge(self.sem, total(self.base + self.n, self.loops))

    def mark(self, instruction):
        instruction.then_inc(self.sem, 1)
        self.n += 1

    @contextmanager
    def loop(self, first, end, per):
        with self.engine.Fori(first, end) as i:
            outer, start = self.loops, self.base + self.n
            enter = start - first * per
            self.base, self.n, self.loops = enter, 0, [*outer, (i, per)]
            yield i
            links = self.base + self.n - enter
            assert links == per, f"links in the loop: {links}"
        self.base, self.loops, self.n = start + (end - first) * per, outer, 0


def hybrid_layer(nc, x, attn_norm, w_in, gdn_conv_w, gdn_a_log, gdn_dt_bias, gdn_norm,
                 lru_conv_w, lru_conv_b, lru_w_a, lru_b_a, lru_w_x, lru_b_x, lru_lambda,
                 w_branch_gdn, w_branch_lru, w_out, mlp_norm, w_up, w_down, final_norm, out):
    ctx = ExitStack()
    with ctx:
        def sb(name, shape, dt=F32, where=ctx):
            return where.enter_context(nc.sbuf_tensor(name, shape, dt))

        def sem(name):
            return ctx.enter_context(nc.semaphore(name))

        w_raw = sb("w_raw", [P, RAW, PIECE])
        w_hi = sb("w_hi", [P, SPLIT, PIECE], F32R)
        w_lo = sb("w_lo", [P, SPLIT, PIECE], F32R)
        act_hi = sb("act_hi", [P, KT * T], F32R)
        act_lo = sb("act_lo", [P, KT * T], F32R)
        ident = sb("ident", [P, P])
        ones = sb("ones", [P, P])
        par = sb("par", [P, ROWS_A])
        conv_par = sb("conv_par", [P, ROWS_B])
        half_ba = sb("half_ba", [P, HEADS])
        half_bx = sb("half_bx", [P, HEADS])
        half_gn = sb("half_gn", [P, 1])
        nsp2 = sb("nsp2", [P, HEADS])
        eps = sb("eps", [P, 1])
        eps4 = sb("eps4", [P, 1])
        eps4q = sb("eps4q", [P, 1])
        lam = sb("lam", [P, 6, HEADS])
        gb_tok = sb("gb_tok", [P, 2, TT, 2 * HEADS])
        y_rs = sb("y_rs", [P, TT])
        sq = sb("sq", [P, T])
        acc = sb("acc", [P, T])
        rstd = sb("rstd", [P, T])
        work = sb("work", [P, 2, T])

        with ExitStack() as first:
            x_tok = [sb(f"x_tok{t}", [P, D], where=first) for t in range(TT)]
            rows_a = sb("rows_a", [ROWS_A, P], where=first)
            rows_b = sb("rows_b", [ROWS_B, P], where=first)
            ss_x = sb("ss_x", [P, TT], where=first)
            rs_x = sb("rs_x", [P, TT], where=first)
            gain_bc = sb("gain_bc", [P, D], where=first)
            w_ab = sb("w_ab", [P, KT * 2 * HEADS], where=first)
            w_ab_hi = sb("w_ab_hi", [P, KT * 2 * HEADS], F32R, where=first)
            w_ab_lo = sb("w_ab_lo", [P, KT * 2 * HEADS], F32R, where=first)
            x_sq = sb("x_sq", [P, D], where=first)
        with ExitStack() as second:
            o_all = sb("o_all", [P, HEADS * T], where=second)
            lru_all = sb("lru_all", [P, HEADS * T], where=second)
            causal = sb("causal", [P, P], where=second)
            level = sb("level", [P, len(LEVELS), P], where=second)
            with ExitStack() as projecting:
                xpad_t = [sb(f"xpad_t{k}", [P, CONV - 1 + T], where=projecting) for k in range(2)]
                y_t = [sb(f"y_t{k}", [P, T], where=projecting) for k in range(2)]
                th_t = [sb(f"th_t{k}", [P, T], where=projecting) for k in range(2)]
                s_t = {k: sb(f"s_t{k}", [P, T], where=projecting) for k in (0, 1, 2, 4)}
                sq_t = [sb(f"sq_t{k}", [P, T], where=projecting) for k in range(4)]
                ab = sb("ab", [2 * HEADS, 10, T], where=projecting)
                rs_t = sb("rs_t", [P, 4 * T], where=projecting)
                s_t |= {k: sb(f"s_t{k}", [P, T], where=projecting) for k in (3, 5)}
            with ExitStack() as units:
                state = sb("state", [P, GH, P], where=units)
                xpad = sb("xpad", [P, CONV - 1 + T], where=units)
                decay, e_g, attn, lt, xs, xts, prod, qd, k_s, kd, rhs, lxr = [
                    sb(n, [P, GH, P], where=units)
                    for n in ("decay", "e_g", "attn", "lt", "xs", "xts", "prod", "qd", "k_s", "kd",
                              "rhs", "lxr")]
                ks, qs, vs, g_bc, b_bc, vnew = [sb(n, [P, GH, P], where=units)
                                                for n in ("ks", "qs", "vs", "g_bc", "b_bc", "vnew")]
                sc = sb("sc", [P, 8, GH], where=units)
                ltm = sb("ltm", [P, 2, GH, P], where=units)
                xc = sb("xc", [P, T], where=units)
                w_ga = sb("w_ga", [P, P], where=units)
                w_gx = sb("w_gx", [P, P], where=units)
                thr, thi, tla, ysb, gel = [sb(n, [P, T], where=units)
                                           for n in ("thr", "thi", "tla", "ysb", "gel")]
                gate_out = sb("gate_out", [P, 2, T], where=units)
        with ExitStack() as third:
            sb("under_o_lru", [P, 2 * HEADS * T], where=third)
            o_hi = sb("o_hi", [P, HEADS * T], F32R, where=third)
            o_lo = sb("o_lo", [P, HEADS * T], F32R, where=third)
            lru_hi = sb("lru_hi", [P, HEADS * T], F32R, where=third)
            lru_lo = sb("lru_lo", [P, HEADS * T], F32R, where=third)
        with ExitStack() as merging:
            gate_in = sb("gate_in", [P, 2, 2, T], where=merging)
            mix = sb("mix", [P, 3, T], where=merging)
        with ExitStack() as fourth:
            x1 = sb("x1", [P, KT * T], where=fourth)
            h2_hi = sb("h2_hi", [P, KT * T], F32R, where=fourth)
            h2_lo = sb("h2_lo", [P, KT * T], F32R, where=fourth)

        ps = ctx.enter_context(nc.psum_tensor("ps", [P, 8, T], F32))

        qkv_dram = nc.dram_tensor("qkv_scratch", (3 * HEADS * P, T), F32, kind="Internal").ap()
        gb_dram = nc.dram_tensor("gb_scratch", (4 * HEADS, T), F32, kind="Internal").ap()
        gate_dram = nc.dram_tensor("gate_scratch", (2 * KT * P, T), F32, kind="Internal").ap()
        qkv_view = qkv_dram.rearrange("(r d) t -> d r t", d=P)

        w_loaded = [sem(f"w_loaded{s}") for s in range(RAW)]
        w_hi_ready = sem("w_hi_ready")
        w_split = [sem(f"w_split{s}") for s in range(RAW)]
        piece_done = [sem(f"piece_done{s}") for s in range(SPLIT)]
        bank_free = [sem(f"bank_free{b}") for b in range(2)]
        const_ready = sem("const_ready")
        masks_ready = sem("masks_ready")
        par_loaded = sem("par_loaded")
        par_t_ready = sem("par_t_ready")
        par_ready = sem("par_ready")
        ab_zero, ab_loaded = sem("ab_zero"), sem("ab_loaded")
        x_loaded = [sem(f"x_loaded{t}") for t in range(TT)]
        gain_loaded, w_ab_loaded = sem("gain_loaded"), sem("w_ab_loaded")
        w_ab_hi_ready, w_ab_ready = sem("w_ab_hi_ready"), sem("w_ab_ready")
        ab_done = sem("ab_done")
        x_ss, x_ms = sem("x_ss"), sem("x_ms")
        x_rs, x_scaled = sem("x_rs"), sem("x_scaled")
        xt_done = sem("xt_done")
        act_hi_ready = sem("act_hi_ready")
        act_ready = sem("act_ready")
        dve_chain, pool_chain = sem("dve_chain"), sem("pool_chain")
        lam_act, lam_dve = sem("lam_act"), sem("lam_dve")
        ab_act, ab_dve = sem("ab_act"), sem("ab_dve")
        ab_t, ab_tok, gb_stored = sem("ab_t"), sem("ab_tok"), sem("gb_stored")
        pad_zero = sem("pad_zero")
        y_ready, th_ready = sem("y_ready"), sem("th_ready")
        s_ready, sq_ready = sem("s_ready"), sem("sq_ready")
        ss_ready, rs_ready = sem("ss_ready"), sem("rs_ready")
        qkv_ready, qkv_dma = sem("qkv_ready"), sem("qkv_dma")
        qkv_stored = sem("qkv_stored")
        early_stored = sem("early_stored")
        unit_in, unit_free = sem("unit_in"), sem("unit_free")
        diff_ready, exp_ready = sem("diff_ready"), sem("exp_ready")
        heads_done, kv_ready = sem("heads_done"), sem("kv_ready")
        ltm_ready = sem("ltm_ready")
        p_done, p_copied = sem("p_done"), sem("p_copied")
        xx_done, x_ready = sem("xx_done"), sem("x_ready")
        xr_done, xr_copied = sem("xr_done"), sem("xr_copied")
        lxr_done, lxr_copied = sem("lxr_done"), sem("lxr_copied")
        vnew_done, vnew_ready = sem("vnew_done"), sem("vnew_ready")
        state_done, state_ready = sem("state_done"), sem("state_ready")
        o_done, o_copied = sem("o_done"), sem("o_copied")
        osq_ready, oss_done = sem("osq_ready"), sem("oss_done")
        ors_ready = sem("ors_ready")
        lru_w_in = sem("lru_w_in")
        xc_ready, lgate_done = sem("xc_ready"), sem("lgate_done")
        lth_ready, tla_ready, rt_ready = sem("lth_ready"), sem("tla_ready"), sem("rt_ready")
        ysb_ready, gin_ready, gth_ready = sem("ysb_ready"), sem("gin_ready"), sem("gth_ready")
        lru_ready = sem("lru_ready")
        gate_dma, gate_free = sem("gate_dma"), [sem(f"gate_free{k}") for k in range(2)]
        z_th, z_mul, z_hi, o_ready = sem("z_th"), sem("z_mul"), sem("z_hi"), sem("o_ready")
        lru_hi_ready, lru_split = sem("lru_hi_ready"), sem("lru_split")
        gate_loaded = [sem(f"gate_loaded{k}") for k in range(2)]
        mix_ready = sem("mix_ready")
        xin_loaded = [sem(f"xin_loaded{k}") for k in range(2)]
        xin_done, xin_copied = sem("xin_done"), sem("xin_copied")
        sq1_ready, acc_done, nss_done = sem("sq1_ready"), sem("acc_done"), sem("nss_done")
        nroot_ready = sem("nroot_ready")
        u_sq, u_hi_ready, u_ready = sem("u_sq"), sem("u_hi_ready"), sem("u_ready")
        y_scaled, y_done, y_copied, y_dma = sem("y_scaled"), sem("y_done"), sem("y_copied"), sem("y_dma")

        block = ctx.enter_context(nc.Block())

        def heads4(tile2d, row0, tok0):
            return tile2d.rearrange("p (h t) -> p h t", t=T)[:, ds(row0, GH), ds(tok0, P)]

        def tile_wait(engine, piece, loops):
            engine.wait_ge(piece_done[piece % SPLIT], uses(piece, loops, SPLIT) + 2)

        def read_wait(engine, tile, loops):
            engine.wait_ge(bank_free[tile % 2], uses(tile, loops, 2) + 2)

        def per_head(column4):
            return column4.unsqueeze(2).to_broadcast([P, GH, P])

        def all_heads(mask):
            return mask.unsqueeze(1).to_broadcast([P, GH, P])

        def x_in(k):
            return work[:, k, :].rearrange("p (t n) -> p t n", t=TT)

        def quad(tile2d, t, q):
            return tile2d.rearrange("p (k t) -> p k t", t=T)[:, 4 * q:4 * q + 4, t * P:(t + 1) * P]

        def flat(tile3d):
            return tile3d[:, :, :].rearrange("p h t -> p (h t)")

        def bank4(b):
            return ps[:, b, :].rearrange("p (h t) -> p h t", h=GH)

        @block.sync
        def _(sp):
            def rows(dst, r0, n, src):
                sp.dma_start(dst[r0:r0 + n, :], src).then_inc(par_loaded, 16)

            for t in range(TT):
                sp.dma_start(x_tok[t][:, :], x[0, t * P:(t + 1) * P, :]).then_inc(x_loaded[t], 16)
                if t == 0:
                    sp.dma_start(gain_bc[:, :], attn_norm[0].partition_broadcast(P)).then_inc(gain_loaded, 16)
                if t == 1:
                    sp.dma_start(w_ab[:, :].rearrange("p (k n) -> p k n", k=KT),
                                 w_in[0].rearrange("(k p) n -> p k n", p=P)[:, :, COL_AB:COL_AB + 2 * HEADS])\
                      .then_inc(w_ab_loaded, 16)
            rows(rows_a, R_ATTN, KT, attn_norm.rearrange("o (k p) -> (o k) p", p=P))
            rows(rows_a, R_MLP, KT, mlp_norm.rearrange("o (k p) -> (o k) p", p=P))
            rows(rows_a, R_FIN, KT, final_norm.rearrange("(k p) -> k p", p=P))
            rows(rows_a, R_LCW, CONV * HEADS, lru_conv_w.rearrange("o j (k p) -> (o j k) p", p=P))
            for r0, src in ((R_LCB, lru_conv_b), (R_BA, lru_b_a), (R_BX, lru_b_x), (R_LAM, lru_lambda)):
                rows(rows_a, r0, HEADS, src.rearrange("o (k p) -> (o k) p", p=P))
            rows(rows_a, R_GN, 1, gdn_norm)
            rows(rows_b, 0, ROWS_B, gdn_conv_w.rearrange("o j (k p) -> (o j k) p", p=P))

            def load(static, loops, weight, k0, col):
                slot = static % RAW
                sp.wait_ge(w_split[slot], uses(static, loops, RAW) + 1)
                src = weight.rearrange("(k p) n -> p k n", p=P)[:, ds(k0, KC), ds(col, P)]
                sp.dma_start(w_raw[:, slot, :].rearrange("p (k n) -> p k n", k=KC), src)\
                  .then_inc(w_loaded[slot], 16)

            sp.wait_ge(ab_zero, 1)
            sp.dma_start(ab[0:HEADS, 9, 0:1], gdn_a_log.rearrange("o h -> h o")).then_inc(ab_loaded, 16)
            sp.dma_start(ab[0:HEADS, 9, 1:2], gdn_dt_bias.rearrange("o h -> h o")).then_inc(ab_loaded, 16)
            with sp.Fori(0, HEADS // 2) as i:
                for j in range(12):
                    t = j // 2
                    col = (COL_V + (t - 4) * P) if t >= 4 else (COL_Q, COL_K)[t % 2] + t // 2 * P
                    load(N_QKV + j, [(i, 12)], w_in[0], j % 2 * KC, i * (2 * P) + col)

            def unit_inputs(g, c):
                sp.wait_ge(gb_stored, 32)
                sp.wait_ge(ab_tok, 1)
                sp.wait_ge(qkv_stored, total(1 + GH // 2, [(g, GH // 2)]))
                sp.wait_ge(unit_free, total(1, [(g, TT), (c, 1)]))
                for dst, kind in ((ks, 1), (qs, 0), (vs, 2)):
                    sp.dma_start(dst[:, :, :], qkv_view[:, ds(g * GH + kind * HEADS, GH), ds(c * P, P)])\
                      .then_inc(unit_in, 16)
                for dst, row in ((g_bc, 0), (b_bc, 3 * HEADS)):
                    sp.dma_start(dst[:, :, :], gb_dram[ds(g * GH + row, GH), ds(c * P, P)]
                                 .partition_broadcast(P)).then_inc(unit_in, 16)
                sp.wait_ge(lgate_done, total(1, [(g, TT), (c, 1)]))
                for dst, src in ((w_ga, lru_w_a), (w_gx, lru_w_x)):
                    sp.dma_start(dst[:, :], src[0].rearrange("n i j -> i n j")
                                 [:, ds(g * TT + c, 1), :].rearrange("i o j -> i (o j)")).then_inc(lru_w_in, 16)

            with sp.Fori(0, GROUPS) as g:
                with sp.Fori(0, TT) as c:
                    for j in range(12):
                        t = j // 2
                        if t < 2:
                            col = c * P + (g * (TT * P) + (COL_XB, COL_YB)[t])
                        else:
                            col = c * (4 * P) + (g * (TT * 4 * P) + (COL_GATE + (t - 2) * P))
                        load(N_UNIT + j, [(g, 48), (c, 12)], w_in[0], j % 2 * KC, col)
                        if j == 2:
                            unit_inputs(g, c)
            with sp.Fori(0, HEADS // 2) as i:
                for j in range(4):
                    load(N_Z + j, [(i, 4)], w_in[0], j % 2 * KC, i * (2 * P) + (COL_Z + j // 2 * P))
            with sp.Fori(0, KT // 2) as i:
                for j in range(4):
                    load(N_MERGE + j, [(i, 4)], (w_branch_lru, w_branch_gdn)[j % 2][0], 0,
                         i * (2 * P) + j // 2 * P)
            with sp.Fori(0, KT // 2) as i:
                for j in range(4):
                    load(N_OUT + j, [(i, 4)], w_out[0], j % 2 * KC, i * (2 * P) + j // 2 * P)
            with sp.Fori(0, FF_PARTS) as part:
                with sp.Fori(0, KT // 2) as i:
                    for j in range(4):
                        load(N_MLP + j, [(part, N_PART), (i, 4)], w_up[0], j % 2 * KC,
                             i * (2 * P) + (part * D + j // 2 * P))
                with sp.Fori(0, KT // 2) as i:
                    for j in range(4):
                        load(N_DOWN + j, [(part, N_PART), (i, 4)], w_down[0],
                             part * KT + j % 2 * KC, i * (2 * P) + j // 2 * P)
            for k in range(KT):
                sp.wait_ge(y_copied, k + 1)
                sp.dma_start(out[0].rearrange("(t p) n -> p t n", p=P)[:, :, k * P:(k + 1) * P],
                             x1[:, k * T:(k + 1) * T].rearrange("p (t n) -> p t n", t=TT)).then_inc(y_dma, 16)
            sp.wait_ge(y_dma, 16 * KT)

        @block.gpsimd
        def _(pool):
            pool_count = Chain(pool, pool_chain)
            nc.gpsimd.memset(ones[:, :], 1.0).then_inc(const_ready, 1)
            pool_count.then(nc.gpsimd.memset(ident[:, :], 0.0))
            nc.gpsimd.affine_select(out=ident[:, :], in_=ident[:, :], compare_op=ALU.not_equal, fill=1.0,
                                    base=0, pattern=[[-1, P]], channel_multiplier=1).then_inc(const_ready, 1)
            pool.wait_ge(xt_done, TT * QUADS)
            pool.wait_ge(par_t_ready, 1)
            pool_count.mark(nc.gpsimd.memset(causal[:, :], 1.0))
            pool_count.then(nc.gpsimd.memset(level[:, :, :], 0.0))
            for n, s in enumerate(LEVELS):
                later = level[:, n, :].rearrange("p (b h r) -> p b h r", h=2, r=s)[:, :, 1, :]
                pool_count.then(nc.gpsimd.memset(later, 1.0))
                pool_count.then(nc.gpsimd.affine_select(
                    out=later, in_=later, compare_op=ALU.is_ge, fill=0.0, base=0,
                    pattern=[[-2 * s, P // (2 * s)], [0, s]], channel_multiplier=1))
                pool_count.then(nc.gpsimd.affine_select(
                    out=later, in_=later, compare_op=ALU.is_ge, fill=0.0, base=s - 1,
                    pattern=[[2 * s, P // (2 * s)], [0, s]], channel_multiplier=-1))
            nc.gpsimd.affine_select(out=causal[:, :], in_=causal[:, :], compare_op=ALU.is_ge, fill=0.0,
                                    base=0, pattern=[[1, P]], channel_multiplier=-1).then_inc(masks_ready, 1)

            pool.wait_ge(ab_dve, 3)
            pool.dma_start(gb_dram[0:2 * HEADS, :], ab[:, 7, :]).then_inc(gb_stored, 16)
            pool.dma_start(gb_dram[2 * HEADS:4 * HEADS, :], ab[:, 8, :]).then_inc(gb_stored, 16)

            def store(t, i, n):
                row = ((2 * HEADS + t - 4) if t >= 4 else (t % 2 * HEADS + t // 2)) * P
                pool.wait_ge(qkv_ready, n)
                if t < 4:
                    pool_count.then(nc.gpsimd.tensor_tensor(s_t[t][:, :], s_t[t][:, :],
                                                            rs_t[:, t * T:(t + 1) * T], ALU.mult))
                pool.dma_start(qkv_dram[ds(i * (2 * P) + row, P), :], s_t[t][:, :]).then_inc(qkv_dma, 16)

            def last_two(i, order):
                for n, t in enumerate(order):
                    store(t, i - 1, i * 6 + (n - 1))
                pool.wait_ge(qkv_dma, i * 96)
                pool.sem_inc(qkv_stored, 1)

            def first_four(i):
                for n, t in enumerate((0, 1, 4, 2)):
                    store(t, i, i * 6 + (n + 1))

            first_four(0)
            with pool_count.loop(1, HEADS // 2, 4) as i:
                last_two(i, (5, 3))
                first_four(i)
            pool.wait_ge(qkv_dma, 16 * (6 * (HEADS // 2) - 2))
            pool.sem_inc(early_stored, 1)
            last_two(HEADS // 2, (3, 5))

            with pool.Fori(0, GROUPS) as g:
                with pool.Fori(0, TT) as c:
                    for k in range(4):
                        read_wait(pool, M_UNIT + 2 + k, [(g, 24), (c, 6)])
                        pool.dma_start(gate_dram[ds(g * (TT * 4 * P) + (c * (4 * P) + k * P), P), :],
                                       gate_out[:, k % 2, :]).then_inc(gate_dma, 16)
                        pool.wait_ge(gate_dma, total(16 * (k + 1), [(g, 64 * TT), (c, 64)]))
                        pool.sem_inc(gate_free[k % 2], 1)

            pool.wait_ge(lru_split, HEADS)
            pool.wait_ge(o_ready, HEADS)
            with pool.Fori(0, KT // 2) as i:
                for k in range(2):
                    pool.wait_ge(mix_ready, total(k + 1, [(i, 2)]))
                    for n in range(2):
                        pool.dma_start(gate_in[:, k, n, :], gate_dram[ds(i * (2 * P) + (n * KT + k) * P, P), :])\
                            .then_inc(gate_loaded[k], 16)
            with pool.Fori(0, KT // 2) as i:
                for k in range(2):
                    pool.wait_ge(xin_done, total(k + 1, [(i, 2)]))
                    pool.dma_start(x_in(k), x[0].rearrange("(t p) n -> p t n", p=P)
                                   [:, :, ds(i * (2 * P) + k * P, P)]).then_inc(xin_loaded[k], 16)

        @block.tensor
        def _(pe):
            for s in piece_done:
                pe.sem_inc(s, 1)
            pe.sem_inc(lgate_done, 1)
            pe.sem_inc(xin_done, 2)

            def half(static, loops, part, a_hi, a_lo, k0, tile, mloops, first, last):
                raw, slot, bank = static % RAW, static % SPLIT, tile % 2
                if part == 0:
                    pe.wait_ge(w_split[raw], uses(static, loops, RAW) + 2)
                    if first:
                        pe.wait_ge(bank_free[bank], uses(tile, mloops, 2) + 1)
                for kk in range(4 * part, 4 * part + 4):
                    cols, w = slice((k0 + kk) * T, (k0 + kk + 1) * T), slice(kk * P, (kk + 1) * P)
                    for n, (wt, a) in enumerate(((w_hi, a_hi), (w_hi, a_lo), (w_lo, a_hi))):
                        mm = nc.tensor.matmul(ps[:, bank, :], wt[:, slot, w], a[:, cols],
                                              start=first and kk == 0 and n == 0,
                                              stop=last and kk == KC - 1 and n == 2)
                if part == 1:
                    mm.then_inc(piece_done[slot], 1)

            def piece(static, loops, a_hi, a_lo, k0, tile, mloops, first=None, last=None, between=()):
                first = k0 == 0 if first is None else first
                last = k0 == KC if last is None else last
                for part in range(2):
                    half(static, loops, part, a_hi, a_lo, k0, tile, mloops, first, last)
                    if part < len(between) and between[part]:
                        between[part]()

            def ab_product(t):
                pe.wait_ge(act_ready, (t + 1) * QUADS)
                for k in range(KT):
                    at, w = slice(k * T + t * P, k * T + (t + 1) * P), slice(k * 2 * HEADS, (k + 1) * 2 * HEADS)
                    for n, (wt, a) in enumerate(((w_ab_hi, act_hi), (w_ab_hi, act_lo), (w_ab_lo, act_hi))):
                        mm = nc.tensor.matmul(ps[0:2 * HEADS, 7, t * P:(t + 1) * P], wt[:, w], a[:, at],
                                              start=k == 0 and n == 0, stop=k == KT - 1 and n == 2)
                mm.then_inc(ab_done, 1)

            pe.wait_ge(const_ready, 2)
            for t in range(TT):
                if t == TT - 1:
                    pe.wait_ge(par_loaded, 16 * 10)
                    nc.tensor.transpose(ps[:, 6, 0:ROWS_A], rows_a[:, :], ident[0:ROWS_A, 0:ROWS_A])
                    nc.tensor.transpose(ps[:, 6, P:P + ROWS_B], rows_b[:, :], ident[0:ROWS_B, 0:ROWS_B])\
                        .then_inc(par_t_ready, 1)
                pe.wait_ge(x_scaled, t + 1)
                for q in range(QUADS):
                    n = t * QUADS + q
                    if n >= 4:
                        pe.wait_ge(act_ready, n - 3)
                    for f in range(4):
                        k = 4 * q + f
                        tr = nc.tensor.transpose(ps[:, 2 + n % 4, f * P:(f + 1) * P],
                                                 x_tok[t][:, k * P:(k + 1) * P], ident[:, :])
                    tr.then_inc(xt_done, 1)
                if t:
                    pe.wait_ge(w_ab_ready, 1)
                    ab_product(t - 1)
            ab_product(TT - 1)

            def ab_columns():
                pe.wait_ge(ab_dve, 3)
                for n in range(2):
                    for c in range(TT):
                        mm = nc.tensor.matmul(ps[:, 7, (n * TT + c) * 16:(n * TT + c + 1) * 16],
                                              ab[:, 7 + n, c * P:(c + 1) * P], ident[0:16, 0:16],
                                              start=True, stop=True)
                mm.then_inc(ab_t, 1)

            with pe.Fori(0, HEADS // 2) as i:
                def sum_squares(t):
                    pe.wait_ge(sq_ready, total(t + 1, [(i, 4)]))
                    nc.tensor.matmul(ps[:, 2 + t, :], ones[:, :], sq_t[t][:, :], start=True, stop=True)\
                        .then_inc(ss_ready, 1)

                for j in range(12):
                    between = [lambda t=(j - 4) // 2: sum_squares(t)] if j in (4, 6, 8, 10) else ()
                    piece(N_QKV + j, [(i, 12)], act_hi, act_lo, j % 2 * KC, M_QKV + j // 2, [(i, 6)],
                          between=between)
            ab_columns()

            with pe.Fori(0, GROUPS) as g:
                with pe.Fori(0, TT) as c:
                    unit, unit5, unit6 = [(g, TT), (c, 1)], [(g, 5 * TT), (c, 5)], [(g, 6 * TT), (c, 6)]

                    def heads(out_bank, lhs, rhs):
                        for h in range(GH):
                            mm = nc.tensor.matmul(bank4(out_bank)[:, h, :], lhs[:, h, :], rhs[:, h, :],
                                                  start=True, stop=True)
                        return mm

                    def step_heads():
                        pe.wait_ge(unit_in, total(80, [(g, 80 * TT), (c, 80)]))
                        pe.wait_ge(state_ready, total(1, unit))
                        pe.wait_ge(ors_ready, total(1, unit))
                        for h in range(GH):
                            nc.tensor.transpose(bank4(B_X)[:, h, :], ks[:, h, :], ident[:, :])
                        for h in range(GH):
                            nc.tensor.transpose(bank4(B_XT)[:, h, :], vs[:, h, :], ident[:, :])
                        heads(B_P, ks, ks)
                        heads(B_R, ks, state)
                        heads(B_S, ks, qs).then_inc(heads_done, 1)

                    def step_p(n):
                        pe.wait_ge(ltm_ready, total(n + 1, unit6))
                        if n:
                            pe.wait_ge(x_ready, total(n, unit5))
                        heads(B_P, ltm[:, n % 2], xs).then_inc(p_done, 1)

                    def step_x(n):
                        pe.wait_ge(p_copied, total(n + 1, unit5))
                        if n == 0:
                            pe.wait_ge(kv_ready, total(1, unit))
                        if n < 4:
                            heads(B_X, xts, prod).then_inc(xx_done, 1)
                        else:
                            heads(B_XT, prod, xts).then_inc(xx_done, 1)

                    def step_xr():
                        pe.wait_ge(x_ready, total(5, unit5))
                        heads(B_X, xts, rhs).then_inc(xr_done, 1)

                    def step_lxr():
                        pe.wait_ge(ltm_ready, total(6, unit6))
                        pe.wait_ge(xr_copied, total(1, unit))
                        heads(B_P, ltm[:, 1], vnew).then_inc(lxr_done, 1)

                    def step_v():
                        pe.wait_ge(lxr_copied, total(1, unit))
                        heads(B_X, xts, lxr).then_inc(vnew_done, 1)

                    def step_o():
                        pe.wait_ge(vnew_ready, total(1, unit))
                        for h in range(GH):
                            nc.tensor.matmul(bank4(B_XT)[:, h, :], state[:, h, :], qd[:, h, :], start=True, stop=False)
                            mm = nc.tensor.matmul(bank4(B_XT)[:, h, :], vnew[:, h, :], attn[:, h, :],
                                                  start=False, stop=True)
                        mm.then_inc(o_done, 1)
                        heads(B_S, kd, vnew).then_inc(state_done, 1)

                    def step_norm():
                        pe.wait_ge(osq_ready, total(1, unit))
                        nc.tensor.matmul(ps[:, B_P, :], ones[:, :], sq[:, :], start=True, stop=True)\
                            .then_inc(oss_done, 1)

                    def step_lru():
                        pe.wait_ge(xc_ready, total(1, unit))
                        pe.wait_ge(lru_w_in, total(32, [(g, 32 * TT), (c, 32)]))
                        nc.tensor.matmul(ps[:, B_R, :], w_ga[:, :], xc[:, :], start=True, stop=True)
                        nc.tensor.matmul(ps[:, B_I, :], w_gx[:, :], xc[:, :], start=True, stop=True)\
                            .then_inc(lgate_done, 1)

                    steps = {5: step_heads, 17: step_xr, 18: step_lxr, 19: step_v, 21: step_o,
                             22: step_norm}
                    for n in range(5):
                        steps[7 + 2 * n] = lambda n=n: step_p(n)
                        if 8 + 2 * n == 10:
                            steps[10] = lambda n=n: (step_x(n), step_lru())
                        else:
                            steps[8 + 2 * n] = lambda n=n: step_x(n)
                    for j in range(12):
                        piece(N_UNIT + j, [(g, 48), (c, 12)], act_hi, act_lo, j % 2 * KC,
                              M_UNIT + j // 2, [(g, 24), (c, 6)], between=(steps.get(2 * j), steps.get(2 * j + 1)))

            with pe.Fori(0, HEADS // 2) as i:
                for j in range(4):
                    piece(N_Z + j, [(i, 4)], act_hi, act_lo, j % 2 * KC, M_Z + j // 2, [(i, 2)])

            pe.wait_ge(lru_split, HEADS)
            with pe.Fori(0, KT // 2) as i:
                for j in range(4):
                    if j % 2 == 1:
                        pe.wait_ge(o_ready, HEADS)
                    a_hi, a_lo = ((lru_hi, lru_lo), (o_hi, o_lo))[j % 2]
                    piece(N_MERGE + j, [(i, 4)], a_hi, a_lo, 0, M_MERGE + j, [(i, 4)], True, True)

            with pe.Fori(0, KT // 2) as i:
                for j in range(4):
                    if j % 2 == 0:
                        k = j // 2
                        pe.wait_ge(xin_loaded[k], total(16, [(i, 16)]))
                        pe.wait_ge(xin_copied, total(k + 1, [(i, 2)]))
                        for t in range(TT):
                            tr = nc.tensor.transpose(ps[:, 2 + k, t * P:(t + 1) * P], x_in(k)[:, t, :], ident[:, :])
                        tr.then_inc(xin_done, 1)
                    pe.wait_ge(act_ready, KT + 8 + 8 * (j % 2))
                    piece(N_OUT + j, [(i, 4)], act_hi, act_lo, j % 2 * KC, M_OUT + j // 2, [(i, 2)])

            def norm_sum():
                pe.wait_ge(acc_done, KT)
                nc.tensor.matmul(ps[:, 4, :], ones[:, :], acc[:, :], start=True, stop=True).then_inc(nss_done, 1)

            def up_pair(part, i, between=()):
                for j in range(4):
                    pe.wait_ge(act_ready, 2 * KT + 8 + 8 * (j % 2))
                    piece(N_MLP + j, [(part, N_PART), (i, 4)], h2_hi, h2_lo, j % 2 * KC,
                          M_MLP + j // 2, [(part, M_PART), (i, 2)], between=between if j == 0 else ())

            def down(part):
                with pe.Fori(0, KT // 2) as i:
                    for j in range(4):
                        pe.wait_ge(u_ready, total(8 + 8 * (j % 2), [(part, KT)]))
                        piece(N_DOWN + j, [(part, N_PART), (i, 4)], act_hi, act_lo, j % 2 * KC,
                              M_DOWN + j // 2, [(part, M_PART), (i, 2)])

            up_pair(0, 0, between=(None, norm_sum))
            with pe.Fori(1, KT // 2) as i:
                up_pair(0, i)
            down(0)
            with pe.Fori(1, FF_PARTS) as part:
                with pe.Fori(0, KT // 2) as i:
                    up_pair(part, i)
                down(part)
            for k in range(KT):
                if k == 2:
                    pe.wait_ge(acc_done, 2 * KT)
                    for t in range(TT):
                        mm = nc.tensor.matmul(ps[:, 6, t:t + 1], acc[:, t * P:(t + 1) * P], ones[:, 0:1],
                                              start=True, stop=True)
                    mm.then_inc(nss_done, 1)
                pe.wait_ge(y_scaled, k + 1)
                if k >= 4:
                    pe.wait_ge(y_copied, k - 3)
                for t in range(TT):
                    tr = nc.tensor.transpose(ps[:, 2 + k % 4, t * P:(t + 1) * P],
                                             x1[:, k * T + t * P:k * T + (t + 1) * P], ident[:, :])
                tr.then_inc(y_done, 1)

        @block.scalar
        def _(act):
            act.sem_inc(ors_ready, 1)
            act.sem_inc(xin_copied, 1)
            run = nc.scalar.activation

            def split(static, loops):
                raw, slot = static % RAW, static % SPLIT
                act.wait_ge(w_loaded[raw], uses(static, loops, RAW) * 16 + 16)
                act.wait_ge(piece_done[slot], uses(static, loops, SPLIT) + 1)
                run(w_hi[:, slot, :], w_raw[:, raw, :], ACT.Copy).then_inc(w_hi_ready, 1)

            def beside(first, count, loops, end=0):
                for j in range(count):
                    yield j
                    if j < count - end:
                        split(first + j + 2, loops)

            def x_root(t):
                act.wait_ge(x_loaded[t], 16)
                if t:
                    act.wait_ge(x_ss, t)
                run(x_sq[:, :], x_tok[t][:, :], ACT.Square, accum_out=ss_x[:, t:t + 1]).then_inc(x_ss, 1)
                act.wait_ge(x_ms, t + 1)
                run(rs_x[:, t:t + 1], rs_x[:, t:t + 1], ACT.Sqrt).then_inc(x_rs, 1)

            def round_h(t):
                for q in range(QUADS):
                    n = t * QUADS + q
                    act.wait_ge(xt_done, n + 1)
                    run(quad(act_hi, t, q), bank4(2 + n % 4), ACT.Copy).then_inc(act_hi_ready, 1)

            for t in range(TT):
                x_root(t)
                if t:
                    round_h(t - 1)
                if t == 1:
                    act.wait_ge(w_ab_loaded, 16)
                    run(w_ab_hi[:, :], w_ab[:, :], ACT.Copy).then_inc(w_ab_hi_ready, 1)
            split(0, [])
            round_h(TT - 1)
            act.wait_ge(par_t_ready, 1)
            run(par[:, :], ps[:, 6, 0:ROWS_A], ACT.Copy).then_inc(par_ready, 1)
            run(conv_par[:, :], ps[:, 6, P:P + ROWS_B], ACT.Copy).then_inc(par_ready, 1)

            def decay_step(j):
                if j == 0:
                    act.wait_ge(ab_done, TT)
                    run(ab[:, 0, :], ps[0:2 * HEADS, 7, :], ACT.Copy).then_inc(ab_act, 1)
                    act.wait_ge(ab_act, 1)
                    run(ab[:, 6, :], ab[:, 0, :], ACT.Tanh, scale=0.5).then_inc(ab_act, 1)
                    act.wait_ge(ab_loaded, 32)
                    run(ab[:, 9, 2:3], ab[:, 9, 0:1], ACT.Exp).then_inc(ab_act, 1)
                    act.wait_ge(ab_dve, 1)
                    run(ab[:, 2, :], ab[:, 1, :], ACT.Abs).then_inc(ab_act, 1)
                    act.wait_ge(ab_act, 4)
                    run(ab[:, 3, :], ab[:, 2, :], ACT.Exp, scale=-1.0).then_inc(ab_act, 1)
                if j == 1:
                    act.wait_ge(ab_dve, 2)
                    run(ab[:, 5, :], ab[:, 4, :], ACT.Ln).then_inc(ab_act, 1)
                if j == 4:
                    act.wait_ge(par_ready, 2)
                    run(lam[:, 0, :], par[:, R_LAM:R_LAM + HEADS], ACT.Abs).then_inc(lam_act, 1)
                    act.wait_ge(lam_act, 1)
                    run(lam[:, 1, :], lam[:, 0, :], ACT.Exp, scale=-1.0).then_inc(lam_act, 1)
                    act.wait_ge(lam_dve, 1)
                    run(lam[:, 3, :], lam[:, 2, :], ACT.Ln).then_inc(lam_act, 1)

            act.wait_ge(pad_zero, 2)

            def tanh_y(t, i):
                act.wait_ge(y_ready, total(t + 1, [(i, 6)]))
                run(th_t[t % 2][:, :], y_t[t % 2][:, :], ACT.Tanh, scale=0.5).then_inc(th_ready, 1)

            def pair(i, first=False):
                for j in range(12):
                    split(N_QKV + j + 1, [(i, 12)])
                    if first:
                        decay_step(j)
                    t = j // 2
                    if j % 2 == 0:
                        if not (first and j == 0):
                            tanh_y(t - 1, i)
                        continue
                    if 1 <= t <= 4:
                        act.wait_ge(s_ready, total(t, [(i, 4)]))
                        run(sq_t[t - 1][:, :], s_t[t - 1][:, :], ACT.Square).then_inc(sq_ready, 1)
                    if t >= 2:
                        n = t - 2
                        act.wait_ge(ss_ready, total(n + 1, [(i, 4)]))
                        run(rs_t[:, n * T:(n + 1) * T], ps[:, 2 + n, :], ACT.Sqrt,
                            scale=(float(P), 1.0)[n % 2], bias=(eps4q, eps4)[n % 2][:, :]).then_inc(rs_ready, 1)
                    tile_wait(act, N_QKV + j, [(i, 12)])
                    run(xpad_t[t % 2][:, CONV - 1:], ps[:, (M_QKV + t) % 2, :], ACT.Copy)\
                        .then_inc(bank_free[(M_QKV + t) % 2], 1)

            pair(0, first=True)
            with act.Fori(1, HEADS // 2) as i:
                pair(i)
            split(N_UNIT + 1, [])
            act.wait_ge(ab_t, 1)
            run(gb_tok[:, :, :, :].rearrange("p a c n -> p (a c n)"), ps[:, 7, 0:P], ACT.Copy).then_inc(ab_tok, 1)
            tanh_y(-1, HEADS // 2)

            with act.Fori(0, GROUPS) as g:
                with act.Fori(0, TT) as c:
                    unit, unit2, unit5 = [(g, TT), (c, 1)], [(g, 2 * TT), (c, 2)], [(g, 5 * TT), (c, 5)]
                    pieces, block_n = [(g, 48), (c, 12)], g * TT + c

                    def gate(k):
                        tile_wait(act, N_UNIT + 5 + 2 * k, pieces)
                        act.wait_ge(gate_free[k % 2], total(k // 2 + 1, unit2))
                        run(gate_out[:, k % 2, :], ps[:, (M_UNIT + k) % 2, :], ACT.Tanh, scale=0.5)\
                            .then_inc(bank_free[(M_UNIT + k) % 2], 1)

                    for j in beside(N_UNIT, 12, pieces):
                        if j == 1:
                            act.wait_ge(diff_ready, total(1, unit))
                            run(decay[:, :, :], decay[:, :, :], ACT.Exp).then_inc(exp_ready, 1)
                            run(e_g[:, :, :], g_bc[:, :, :], ACT.Exp).then_inc(exp_ready, 1)
                            run(sc[:, 3:6, :], sc[:, 0:3, :], ACT.Exp).then_inc(exp_ready, 1)
                            tile_wait(act, N_UNIT + 1, pieces)
                            run(xpad[:, CONV - 1:], ps[:, M_UNIT % 2, :], ACT.Copy)\
                                .then_inc(bank_free[M_UNIT % 2], 1)
                        if j == 3:
                            tile_wait(act, N_UNIT + 3, pieces)
                            act.wait_ge(qkv_stored, 1 + HEADS // 2)
                            run(ysb[:, :], ps[:, (M_UNIT + 1) % 2, :], ACT.Copy).then_inc(ysb_ready, 1)
                            run(gel[:, :], ps[:, (M_UNIT + 1) % 2, :], ACT.Square)\
                                .then_inc(bank_free[(M_UNIT + 1) % 2], 1)
                        if j == 5:
                            act.wait_ge(gin_ready, total(1, unit))
                            run(gel[:, :], gel[:, :], ACT.Tanh, scale=GELU_SCALE).then_inc(gth_ready, 1)
                            act.wait_ge(lgate_done, total(2, unit))
                            run(thr[:, :], ps[:, B_R, :], ACT.Tanh, scale=0.5, bias=half_ba[:, ds(block_n, 1)])\
                                .then_inc(lth_ready, 1)
                            run(thi[:, :], ps[:, B_I, :], ACT.Tanh, scale=0.5, bias=half_bx[:, ds(block_n, 1)])\
                                .then_inc(lth_ready, 1)
                        if j == 6:
                            act.wait_ge(lth_ready, total(2, unit2))
                            run(tla[:, :], thr[:, :], ACT.Tanh, scale=nsp2[:, ds(block_n, 1)],
                                bias=nsp2[:, ds(block_n, 1)]).then_inc(tla_ready, 1)
                        if j == 11:
                            act.wait_ge(oss_done, total(1, unit))
                            run(rstd[:, :], ps[:, B_P, :], ACT.Sqrt, scale=1.0 / P, bias=eps[:, :])\
                                .then_inc(ors_ready, 1)
                        if j == 9:
                            act.wait_ge(lxr_done, total(1, unit))
                            run(lxr[:, :, :], bank4(B_P), ACT.Copy).then_inc(lxr_copied, 1)
                        if j in (5, 7, 9, 11):
                            gate((j - 5) // 2)
                        if 3 <= j <= 7:
                            act.wait_ge(p_done, total(j - 2, unit5))
                            run(prod[:, :, :], bank4(B_P), ACT.Copy).then_inc(p_copied, 1)
                        if j == 7:
                            act.wait_ge(tla_ready, total(1, unit))
                            run(thr[:, :], tla[:, :], ACT.Sqrt, scale=-1.0).then_inc(rt_ready, 1)
                        if j == 8:
                            act.wait_ge(xr_done, total(1, unit))
                            run(vnew[:, :, :], bank4(B_X), ACT.Copy).then_inc(xr_copied, 1)
                        if j == 10:
                            act.wait_ge(o_done, total(1, unit))
                            run(prod[:, :, :], bank4(B_XT), ACT.Copy).then_inc(o_copied, 1)
                            act.wait_ge(o_copied, total(1, unit))
                            run(sq[:, :], prod[:, :, :].rearrange("p h t -> p (h t)"), ACT.Square)\
                                .then_inc(osq_ready, 1)

            for k in range(2):
                act.wait_ge(gate_free[k], 1 + 2 * GROUPS * TT)
            with act.Fori(0, HEADS // 2) as i:
                for j in beside(N_Z, 4, [(i, 4)]):
                    if j % 2 == 1:
                        k = j // 2
                        at = ds(i * (2 * T) + k * T, T)
                        tile_wait(act, N_Z + j, [(i, 4)])
                        run(work[:, 0, :], ps[:, (M_Z + k) % 2, :], ACT.Tanh, scale=0.5).then_inc(z_th, 1)
                        act.wait_ge(z_mul, total(k + 1, [(i, 2)]))
                        run(o_hi[:, at], work[:, 1, :], ACT.Copy, scale=half_gn[:, :]).then_inc(z_hi, 1)
                    if j in (1, 2):
                        at = ds(i * (2 * T) + (j - 1) * T, T)
                        act.wait_ge(lru_ready, HEADS)
                        run(lru_hi[:, at], lru_all[:, at], ACT.Copy).then_inc(lru_hi_ready, 1)

            with act.Fori(0, KT // 2) as i:
                for j in beside(N_MERGE, 4, [(i, 4)]):
                    if j % 2 == 1:
                        k = j // 2
                        act.wait_ge(mix_ready, total(k + 3, [(i, 2)]))
                        run(act_hi[:, ds(i * (2 * T) + k * T, T)], mix[:, 2, :], ACT.Copy, scale=0.5)\
                            .then_inc(act_hi_ready, 1)

            with act.Fori(0, KT // 2) as i:
                for j in beside(N_OUT, 4, [(i, 4)]):
                    k = j // 2
                    at = ds(i * (2 * T) + k * T, T)
                    if j % 2 == 0:
                        act.wait_ge(xin_done, total(k + 3, [(i, 2)]))
                        run(x1[:, at], ps[:, 2 + k, :], ACT.Copy).then_inc(xin_copied, 1)
                    else:
                        read_wait(act, M_OUT + k, [(i, 2)])
                        run(h2_hi[:, at], x1[:, at], ACT.Copy, scale=par[:, ds(i * 2 + (R_MLP + k), 1)])\
                            .then_inc(act_hi_ready, 1)
                        run(sq[:, :], x1[:, at], ACT.Square).then_inc(sq1_ready, 1)

            def up_pair(part, i, first=False):
                for j in beside(N_MLP, 4, [(part, N_PART), (i, 4)]):
                    if first and j == 0:
                        act.wait_ge(nss_done, 1)
                        run(rstd[:, :], ps[:, 4, :], ACT.Sqrt, scale=1.0 / D, bias=eps[:, :]).then_inc(nroot_ready, 1)
                    if j % 2 == 1:
                        k = j // 2
                        read_wait(act, M_MLP + k, [(part, M_PART), (i, 2)])
                        run(act_hi[:, ds(i * (2 * T) + k * T, T)], work[:, k, :], ACT.Square).then_inc(u_hi_ready, 1)

            def down(part, i, last_part=False, end=False):
                for j in beside(N_DOWN, 4, [(part, N_PART), (i, 4)], 2 if end else 0):
                    if last_part and j % 2 == 1:
                        k = j // 2
                        read_wait(act, M_DOWN + k, [(part, M_PART), (i, 2)])
                        run(sq[:, :], x1[:, ds(i * (2 * T) + k * T, T)], ACT.Square).then_inc(sq1_ready, 1)

            up_pair(0, 0, first=True)
            with act.Fori(1, KT // 2) as i:
                up_pair(0, i)
            with act.Fori(0, KT // 2) as i:
                down(0, i)
            with act.Fori(1, FF_PARTS - 1) as part:
                with act.Fori(0, KT // 2) as i:
                    up_pair(part, i)
                with act.Fori(0, KT // 2) as i:
                    down(part, i)
            with act.Fori(0, KT // 2) as i:
                up_pair(FF_PARTS - 1, i)
            with act.Fori(0, KT // 2 - 1) as i:
                down(FF_PARTS - 1, i, last_part=True)
            down(FF_PARTS - 1, KT // 2 - 1, last_part=True, end=True)

            act.wait_ge(nss_done, 2)
            run(y_rs[:, :], ps[:, 6, 0:TT], ACT.Sqrt, scale=1.0 / D, bias=eps[:, :]).then_inc(nroot_ready, 1)

        @block.vector
        def _(dve):
            chain = Chain(dve, dve_chain)
            for s in (*w_split, *bank_free, qkv_stored, unit_free, state_ready, *gate_free):
                dve.sem_inc(s, 1)
            dve.sem_inc(mix_ready, 2)
            tt, ts, stt = nc.vector.tensor_tensor, nc.vector.tensor_scalar, nc.vector.scalar_tensor_tensor

            def split(static, loops):
                raw, slot = static % RAW, static % SPLIT
                dve.wait_ge(w_hi_ready, total(static + 1, loops))
                tt(w_lo[:, slot, :], w_raw[:, raw, :], w_hi[:, slot, :].bitcast(F32), ALU.subtract)\
                    .then_inc(w_split[raw], 1)

            def beside(first, count, loops, end=0):
                for j in range(count):
                    yield j
                    if j < count - end:
                        split(first + j + 2, loops)

            def conv(y, padded, weights, col, bias=None):
                def weight(n):
                    return weights[:, ds(col(n), 1)]
                chain.then(ts(y, padded[:, 0:T], weight(0), bias, ALU.mult, ALU.add) if bias is not None
                           else ts(y, padded[:, 0:T], weight(0), None, ALU.mult))
                for n in range(1, CONV):
                    last = stt(out=y, in0=padded[:, n:n + T], scalar=weight(n), in1=y, op0=ALU.mult, op1=ALU.add)
                    if n < CONV - 1:
                        chain.then(last)
                return last

            def log1p_reciprocal(e, u, t):
                chain.then(ts(t, u, -1.0, None, ALU.add))
                chain.then(tt(t, e, t, ALU.subtract))
                chain.then(nc.vector.reciprocal(u, u))

            def log1p_sum(l, u, t):
                chain.then(tt(t, t, u, ALU.mult))
                chain.then(tt(l, l, t, ALU.add))

            nc.vector.memset(eps[:, :], RMS_EPS)
            nc.vector.memset(eps4q[:, :], 4 * L2_EPS * P)
            chain.then(nc.vector.memset(eps4[:, :], 4 * L2_EPS))
            nc.vector.memset(ab[:, 9, :], 0.0).then_inc(ab_zero, 1)

            def rest_of_h(t):
                for q in range(QUADS):
                    n = t * QUADS + q
                    dve.wait_ge(act_hi_ready, n + 1)
                    tt(quad(act_lo, t, q), bank4(2 + n % 4), quad(act_hi, t, q).bitcast(F32), ALU.subtract)\
                        .then_inc(act_ready, 1)

            dve.wait_ge(gain_loaded, 16)
            for t in range(TT):
                dve.wait_ge(x_ss, t + 1)
                chain.then(ts(rs_x[:, t:t + 1], ss_x[:, t:t + 1], 1.0 / D, RMS_EPS, ALU.mult, ALU.add))
                nc.vector.reciprocal(rs_x[:, t:t + 1], rs_x[:, t:t + 1]).then_inc(x_ms, 1)
                dve.wait_ge(x_rs, t + 1)
                stt(out=x_tok[t][:, :], in0=x_tok[t][:, :], scalar=rs_x[:, t:t + 1], in1=gain_bc[:, :],
                    op0=ALU.mult, op1=ALU.mult).then_inc(x_scaled, 1)
                if t:
                    rest_of_h(t - 1)
                if t == 1:
                    dve.wait_ge(w_ab_hi_ready, 1)
                    tt(w_ab_lo[:, :], w_ab[:, :], w_ab_hi[:, :].bitcast(F32), ALU.subtract).then_inc(w_ab_ready, 1)
            split(0, [])
            rest_of_h(TT - 1)
            for xp in xpad_t:
                nc.vector.memset(xp[:, 0:CONV - 1], 0.0).then_inc(pad_zero, 1)
            dve.wait_ge(pad_zero, 2)

            def decay_step(j):
                if j == 0:
                    dve.wait_ge(ab_act, 1)
                    dve.wait_ge(ab_loaded, 32)
                    ts(ab[:, 1, :], ab[:, 0, :], ab[:, 9, 1:2], None, ALU.add).then_inc(ab_dve, 1)
                if j == 1:
                    dve.wait_ge(ab_act, 5)
                    ts(ab[:, 4, :], ab[:, 3, :], 1.0, None, ALU.add).then_inc(ab_dve, 1)
                    chain.then(ts(ab[:, 1, :], ab[:, 1, :], 0.0, None, ALU.max))
                    chain.then(ts(ab[:, 9, 2:3], ab[:, 9, 2:3], -1.0, None, ALU.mult))
                    dve.wait_ge(ab_act, 6)
                    log1p_reciprocal(ab[:, 3, :], ab[:, 4, :], ab[:, 2, :])
                if j == 2:
                    log1p_sum(ab[:, 5, :], ab[:, 4, :], ab[:, 2, :])
                    chain.then(tt(ab[:, 5, :], ab[:, 5, :], ab[:, 1, :], ALU.add))
                    chain.then(ts(ab[:, 5, :], ab[:, 5, :], ab[:, 9, 2:3], None, ALU.mult))
                if j == 3:
                    for c in range(TT):
                        cols = slice(c * P, (c + 1) * P)
                        nc.vector.tensor_tensor_scan(ab[:, 7, cols], ones[0:2 * HEADS, :], ab[:, 5, cols], 0.0,
                                                     ALU.mult, ALU.add)
                    ts(ab[:, 8, :], ab[:, 6, :], 0.5, 0.5, ALU.mult, ALU.add).then_inc(ab_dve, 1)
                if j == 4:
                    dve.wait_ge(lam_act, 2)
                    ts(lam[:, 2, :], lam[:, 1, :], 1.0, None, ALU.add).then_inc(lam_dve, 1)
                    ts(half_ba[:, :], par[:, R_BA:R_BA + HEADS], 0.5, None, ALU.mult)
                    ts(half_bx[:, :], par[:, R_BX:R_BX + HEADS], 0.5, None, ALU.mult)
                    ts(half_gn[:, :], par[:, R_GN:R_GN + 1], 0.5, None, ALU.mult)
                    dve.wait_ge(lam_act, 3)
                    log1p_reciprocal(lam[:, 1, :], lam[:, 2, :], lam[:, 4, :])
                    log1p_sum(lam[:, 3, :], lam[:, 2, :], lam[:, 4, :])
                    chain.then(ts(lam[:, 5, :], par[:, R_LAM:R_LAM + HEADS], -1.0, 0.0, ALU.mult, ALU.max))
                    chain.then(tt(lam[:, 3, :], lam[:, 3, :], lam[:, 5, :], ALU.add))
                    chain.then(ts(nsp2[:, :], lam[:, 3, :], -2.0, None, ALU.mult))

            def convolve(t, i):
                kind, head = (2, t - 4) if t >= 4 else (2, -1) if t < 0 else (t % 2, t // 2)
                read_wait(dve, M_QKV + t, [(i, 6)])
                conv(y_t[t % 2][:, :], xpad_t[t % 2], conv_par,
                     lambda n: i * 2 + (n * 3 * HEADS + kind * HEADS + head)).then_inc(y_ready, 1)

            def silu2(t, i):
                dve.wait_ge(y_ready, total(t + 1, [(i, 6)]))
                dve.wait_ge(th_ready, total(t + 1, [(i, 6)]))
                return stt(out=s_t[t % 6][:, :], in0=th_t[t % 2][:, :], scalar=1.0, in1=y_t[t % 2][:, :],
                           op0=ALU.add, op1=ALU.mult)

            def over_norm(n, i):
                dve.wait_ge(rs_ready, total(n + 1, [(i, 4)]))
                cols = slice(n % 4 * T, (n % 4 + 1) * T)
                nc.vector.reciprocal(rs_t[:, cols], rs_t[:, cols]).then_inc(qkv_ready, 1)

            def pair(i, first=False):
                for j in range(12):
                    split(N_QKV + j + 1, [(i, 12)])
                    if j % 2 == 0:
                        if not (first and j == 0):
                            convolve(j // 2 - 1, i)
                    elif j == 1:
                        if not first:
                            silu2(-1, i).then_inc(qkv_ready, 1)
                            over_norm(-1, i)
                    else:
                        t = (j - 3) // 2
                        if j == 3:
                            dve.wait_ge(qkv_stored, total(1, [(i, 1)]))
                        silu2(t, i).then_inc(s_ready if t < 4 else qkv_ready, 1)
                        if t >= 2:
                            over_norm(t - 2, i)
                    if first:
                        decay_step(j)

            pair(0, first=True)
            with chain.loop(1, HEADS // 2, 18) as i:
                pair(i)
            split(N_UNIT + 1, [])
            convolve(-1, HEADS // 2)
            over_norm(-1, HEADS // 2)
            silu2(-1, HEADS // 2).then_inc(qkv_ready, 1)

            dve.wait_ge(masks_ready, 1)
            chain.then(nc.vector.memset(xpad[:, 0:CONV - 1], 0.0))
            with chain.loop(0, GROUPS, 1 + TT * UNIT_LINKS) as g:
                chain.mark(nc.vector.memset(state[:, :, :], 0.0))
                with chain.loop(0, TT, UNIT_LINKS) as c:
                    unit, unit3, unit5 = [(g, TT), (c, 1)], [(g, 3 * TT), (c, 3)], [(g, 5 * TT), (c, 5)]
                    pieces, block_n = [(g, 48), (c, 12)], g * TT + c

                    def level_mask(n):
                        tt(ltm[:, n % 2, :, :], lt[:, :, :], all_heads(level[:, n + 1, :]), ALU.mult)\
                            .then_inc(ltm_ready, 1)

                    for j in beside(N_UNIT, 12, pieces):
                        if j == 1:
                            dve.wait_ge(unit_in, total(80, [(g, 80 * TT), (c, 80)]))
                            dve.wait_ge(early_stored, 1)
                            g_col = gb_tok[:, 0, ds(c, 1), ds(g * GH, GH)]
                            b_col = gb_tok[:, 1, ds(c, 1), ds(g * GH + HEADS, GH)]
                            nc.vector.tensor_copy(sc[:, 1:2, :], g_col)
                            ts(sc[:, 6:7, :], b_col, 0.5, None, ALU.mult)
                            chain.then(nc.vector.tensor_copy(sc[:, 2:3, :].rearrange("p o h -> p h o"),
                                                             g_bc[:, :, P - 1:P]))
                            tt(sc[:, 0, :], sc[:, 2, :], sc[:, 1, :], ALU.subtract)
                            chain.then(tt(decay[:, :, :], g_bc[:, :, :], per_head(sc[:, 1, :]), ALU.subtract))
                            ts(decay[:, :, :], decay[:, :, :], 0.0, None, ALU.min).then_inc(diff_ready, 1)
                        if j == 2:
                            dve.wait_ge(exp_ready, total(3, unit3))
                            stt(out=sc[:, 7, :], in0=sc[:, 6, :], scalar=-2.0, in1=sc[:, 4, :],
                                op0=ALU.mult, op1=ALU.mult)
                            tt(qd[:, :, :], qs[:, :, :], e_g[:, :, :], ALU.mult)
                            chain.then(tt(decay[:, :, :], decay[:, :, :], all_heads(causal[:, :]), ALU.mult))
                            chain.then(tt(e_g[:, :, :], decay[:, :, :], b_bc[:, :, :], ALU.mult))
                            read_wait(dve, M_UNIT, [(g, 24), (c, 6)])
                            conv(xc[:, :], xpad, par, lambda n: g * TT + (c + (R_LCW + n * HEADS)),
                                 bias=par[:, ds(g * TT + (c + R_LCB), 1)]).then_inc(xc_ready, 1)
                        if j == 3:
                            dve.wait_ge(heads_done, total(1, unit))
                            tt(lt[:, :, :], bank4(B_P), e_g[:, :, :], ALU.mult).then_inc(unit_free, 1)
                            dve.wait_ge(unit_free, total(2, unit))
                            chain.then(tt(xts[:, :, :], lt[:, :, :], all_heads(level[:, 0, :]), ALU.mult))
                            chain.then(tt(xts[:, :, :], all_heads(ident[:, :]), xts[:, :, :], ALU.subtract))
                            nc.vector.transpose(flat(xs), flat(xts))
                            level_mask(0)
                            tt(kd[:, :, :], bank4(B_X), per_head(sc[:, 3, :]), ALU.mult)
                            tt(k_s[:, :, :], bank4(B_R), per_head(sc[:, 7, :]), ALU.mult)
                            tt(rhs[:, :, :], bank4(B_XT), per_head(sc[:, 6, :]), ALU.mult).then_inc(kv_ready, 1)
                            tt(attn[:, :, :], bank4(B_S), decay[:, :, :], ALU.mult)
                        if 4 <= j <= 8:
                            n = j - 4
                            level_mask(n + 1)
                            dve.wait_ge(xx_done, total(n + 1, unit5))
                            if n < 4:
                                chain.then(tt(xs[:, :, :], xs[:, :, :], bank4(B_X), ALU.subtract))
                                nc.vector.transpose(flat(xts), flat(xs)).then_inc(x_ready, 1)
                            else:
                                tt(xts[:, :, :], xts[:, :, :], bank4(B_XT), ALU.subtract).then_inc(x_ready, 1)
                        if j == 4:
                            dve.wait_ge(kv_ready, total(1, unit))
                            chain.mark(tt(rhs[:, :, :], rhs[:, :, :], k_s[:, :, :], ALU.add))
                            dve.wait_ge(ysb_ready, total(1, unit))
                            read_wait(dve, M_UNIT + 1, [(g, 24), (c, 6)])
                            chain.then(ts(gel[:, :], gel[:, :], GELU_CUBIC, 1.0, ALU.mult, ALU.add))
                            tt(gel[:, :], gel[:, :], ysb[:, :], ALU.mult).then_inc(gin_ready, 1)
                        if j == 6:
                            dve.wait_ge(gth_ready, total(1, unit))
                            chain.then(stt(out=ysb[:, :], in0=gel[:, :], scalar=1.0, in1=ysb[:, :],
                                           op0=ALU.add, op1=ALU.mult))
                        if j == 7:
                            dve.wait_ge(tla_ready, total(1, unit))
                            chain.then(ts(gel[:, :], tla[:, :], -1.0, 1.0, ALU.mult, ALU.add))
                            chain.then(nc.vector.reciprocal(gel[:, :], gel[:, :]))
                            chain.then(stt(out=thi[:, :], in0=thi[:, :], scalar=1.0, in1=xc[:, :],
                                           op0=ALU.add, op1=ALU.mult))
                            chain.then(tt(thi[:, :], thi[:, :], gel[:, :], ALU.mult))
                        if j == 8:
                            dve.wait_ge(rt_ready, total(1, unit))
                            tt(thi[:, :], thi[:, :], thr[:, :], ALU.mult)
                            chain.then(stt(out=tla[:, :], in0=tla[:, :], scalar=1.0, in1=gel[:, :],
                                           op0=ALU.add, op1=ALU.mult))
                            chain.then(nc.vector.tensor_tensor_scan(gel[:, :], tla[:, :], thi[:, :], 0.0,
                                                                    ALU.mult, ALU.add))
                            stt(out=lru_all[:, ds(block_n * T, T)], in0=gel[:, :], scalar=0.5, in1=ysb[:, :],
                                op0=ALU.mult, op1=ALU.mult).then_inc(lru_ready, 1)
                        if j == 10:
                            dve.wait_ge(vnew_done, total(1, unit))
                            tt(vnew[:, :, :], vnew[:, :, :], bank4(B_X), ALU.subtract).then_inc(vnew_ready, 1)
                            dve.wait_ge(state_done, total(1, unit))
                            for h in range(GH):
                                last = stt(out=state[:, h, :], in0=state[:, h, :], scalar=sc[:, 5, h:h + 1],
                                           in1=bank4(B_S)[:, h, :], op0=ALU.mult, op1=ALU.add)
                            last.then_inc(state_ready, 1)
                        if j == 11:
                            dve.wait_ge(ors_ready, total(2, unit))
                            chain.then(nc.vector.reciprocal(rstd[:, :], rstd[:, :]))
                            chain.then(tt(heads4(o_all[:, :], g * GH, c * P), prod[:, :, :],
                                          rstd[:, :].rearrange("p (h t) -> p h t", h=GH), ALU.mult))

            for k in range(2):
                dve.wait_ge(gate_free[k], 1 + 2 * GROUPS * TT)
            with dve.Fori(0, HEADS // 2) as i:
                for j in beside(N_Z, 4, [(i, 4)]):
                    if j % 2 == 1:
                        k = j // 2
                        at = ds(i * (2 * T) + k * T, T)
                        dve.wait_ge(z_th, total(k + 1, [(i, 2)]))
                        stt(out=work[:, 1, :], in0=work[:, 0, :], scalar=1.0, in1=ps[:, (M_Z + k) % 2, :],
                            op0=ALU.add, op1=ALU.mult).then_inc(bank_free[(M_Z + k) % 2], 1)
                        read_wait(dve, M_Z + k, [(i, 2)])
                        tt(work[:, 1, :], work[:, 1, :], o_all[:, at], ALU.mult).then_inc(z_mul, 1)
                        dve.wait_ge(z_hi, total(k + 1, [(i, 2)]))
                        stt(out=o_lo[:, at], in0=work[:, 1, :], scalar=half_gn[:, :],
                            in1=o_hi[:, at].bitcast(F32), op0=ALU.mult, op1=ALU.subtract).then_inc(o_ready, 1)
                    if j in (1, 2):
                        at = ds(i * (2 * T) + (j - 1) * T, T)
                        dve.wait_ge(lru_hi_ready, total(j, [(i, 2)]))
                        tt(lru_lo[:, at], lru_all[:, at], lru_hi[:, at].bitcast(F32), ALU.subtract)\
                            .then_inc(lru_split, 1)

            with dve.Fori(0, KT // 2) as i:
                for j in beside(N_MERGE, 4, [(i, 4)]):
                    k, n = j // 2, j % 2
                    dve.wait_ge(gate_loaded[k], total(32, [(i, 32)]))
                    tile_wait(dve, N_MERGE + j, [(i, 4)])
                    stt(out=mix[:, n, :], in0=gate_in[:, k, 1 - n, :], scalar=1.0, in1=ps[:, (M_MERGE + j) % 2, :],
                        op0=ALU.add, op1=ALU.mult).then_inc(bank_free[(M_MERGE + j) % 2], 1)
                    if n == 1:
                        at = ds(i * (2 * T) + k * T, T)
                        read_wait(dve, M_MERGE + j, [(i, 4)])
                        tt(mix[:, 2, :], mix[:, 0, :], mix[:, 1, :], ALU.add).then_inc(mix_ready, 1)
                        dve.wait_ge(act_hi_ready, total(KT + k + 1, [(i, 2)]))
                        stt(out=act_lo[:, at], in0=mix[:, 2, :], scalar=0.5, in1=act_hi[:, at].bitcast(F32),
                            op0=ALU.mult, op1=ALU.subtract).then_inc(act_ready, 1)

            chain.then(nc.vector.memset(acc[:, :], 0.0))
            with dve.Fori(0, KT // 2) as i:
                for j in beside(N_OUT, 4, [(i, 4)]):
                    if j % 2 == 1:
                        k = j // 2
                        at = ds(i * (2 * T) + k * T, T)
                        tile_wait(dve, N_OUT + j, [(i, 4)])
                        dve.wait_ge(xin_copied, total(k + 2, [(i, 2)]))
                        tt(x1[:, at], x1[:, at], ps[:, (M_OUT + k) % 2, :], ALU.add)\
                            .then_inc(bank_free[(M_OUT + k) % 2], 1)
                        read_wait(dve, M_OUT + k, [(i, 2)])
                        dve.wait_ge(act_hi_ready, total(2 * KT + k + 1, [(i, 2)]))
                        stt(out=h2_lo[:, at], in0=x1[:, at], scalar=par[:, ds(i * 2 + (R_MLP + k), 1)],
                            in1=h2_hi[:, at].bitcast(F32), op0=ALU.mult, op1=ALU.subtract).then_inc(act_ready, 1)
                        dve.wait_ge(sq1_ready, total(k + 1, [(i, 2)]))
                        tt(acc[:, :], acc[:, :], sq[:, :], ALU.add).then_inc(acc_done, 1)
                        dve.wait_ge(acc_done, total(k + 1, [(i, 2)]))

            def up_pair(part, i, first=False):
                for j in beside(N_MLP, 4, [(part, N_PART), (i, 4)]):
                    if first and j == 0:
                        dve.wait_ge(nroot_ready, 1)
                        chain.then(nc.vector.reciprocal(rstd[:, :], rstd[:, :]))
                    if j % 2 == 1:
                        k = j // 2
                        at = ds(i * (2 * T) + k * T, T)
                        tile_wait(dve, N_MLP + j, [(part, N_PART), (i, 4)])
                        stt(out=work[:, k, :], in0=ps[:, (M_MLP + k) % 2, :], scalar=0.0, in1=rstd[:, :],
                            op0=ALU.max, op1=ALU.mult).then_inc(bank_free[(M_MLP + k) % 2], 1)
                        read_wait(dve, M_MLP + k, [(part, M_PART), (i, 2)])
                        tt(sq[:, :], work[:, k, :], work[:, k, :], ALU.mult).then_inc(u_sq, 1)
                        dve.wait_ge(u_sq, total(k + 1, [(part, KT), (i, 2)]))
                        dve.wait_ge(u_hi_ready, total(k + 1, [(part, KT), (i, 2)]))
                        tt(act_lo[:, at], sq[:, :], act_hi[:, at].bitcast(F32), ALU.subtract).then_inc(u_ready, 1)

            def down(part, i, last_part=False, end=False):
                for j in beside(N_DOWN, 4, [(part, N_PART), (i, 4)], 2 if end else 0):
                    if j % 2 == 1:
                        k = j // 2
                        at = ds(i * (2 * T) + k * T, T)
                        tile_wait(dve, N_DOWN + j, [(part, N_PART), (i, 4)])
                        tt(x1[:, at], x1[:, at], ps[:, (M_DOWN + k) % 2, :], ALU.add)\
                            .then_inc(bank_free[(M_DOWN + k) % 2], 1)
                        if last_part:
                            dve.wait_ge(sq1_ready, total(KT + k + 1, [(i, 2)]))
                            tt(acc[:, :], acc[:, :], sq[:, :], ALU.add).then_inc(acc_done, 1)
                            read_wait(dve, M_DOWN + k, [(part, M_PART), (i, 2)])
                            ts(x1[:, at], x1[:, at], par[:, ds(i * 2 + (R_FIN + k), 1)], None, ALU.mult)\
                                .then_inc(y_scaled, 1)
                            dve.wait_ge(acc_done, total(KT + k + 1, [(i, 2)]))

            up_pair(0, 0, first=True)
            with dve.Fori(1, KT // 2) as i:
                up_pair(0, i)
            with dve.Fori(0, KT // 2) as i:
                down(0, i)
            with dve.Fori(1, FF_PARTS - 1) as part:
                with dve.Fori(0, KT // 2) as i:
                    up_pair(part, i)
                with dve.Fori(0, KT // 2) as i:
                    down(part, i)
            with dve.Fori(0, KT // 2) as i:
                up_pair(FF_PARTS - 1, i)
            chain.then(nc.vector.memset(acc[:, :], 0.0))
            with dve.Fori(0, KT // 2 - 1) as i:
                down(FF_PARTS - 1, i, last_part=True)
            down(FF_PARTS - 1, KT // 2 - 1, last_part=True, end=True)

            dve.wait_ge(nroot_ready, 2)
            chain.then(nc.vector.reciprocal(y_rs[:, :], y_rs[:, :]))
            for k in range(KT):
                dve.wait_ge(y_done, k + 1)
                tt(x1[:, k * T:(k + 1) * T].rearrange("p (t n) -> p t n", t=TT), bank4(2 + k % 4),
                   per_head(y_rs[:, :]), ALU.mult).then_inc(y_copied, 1)


_INS = ['x', 'attn_norm', 'w_in', 'gdn_conv_w', 'gdn_a_log', 'gdn_dt_bias', 'gdn_norm', 'lru_conv_w',
        'lru_conv_b', 'lru_w_a', 'lru_b_a', 'lru_w_x', 'lru_b_x', 'lru_lambda', 'w_branch_gdn',
        'w_branch_lru', 'w_out', 'mlp_norm', 'w_up', 'w_down', 'final_norm']


def kernel(**inputs):
    import numpy as _np
    import concourse.bacc as _bacc
    from concourse import mybir as _mybir
    from concourse.bass_utils import run_bass_kernel_spmd as _run

    nc = _bacc.Bacc("TRN2", target_bir_lowering=False, num_devices=1)
    arrays, args = {}, []
    for name in _INS:
        a = _np.ascontiguousarray(inputs[name])
        arrays[f"in_{name}_dram"] = a
        args.append(nc.dram_tensor(f"in_{name}_dram", a.shape, _mybir.dt.from_np(a.dtype), kind="ExternalInput").ap())
    result = nc.dram_tensor("out_dram", (1, T, D), F32, kind="ExternalOutput").ap()
    hybrid_layer(nc, *args, result)
    r = _run(nc, [arrays], core_ids=[0])
    return r.results[0]["out_dram"]
```
